# Optimizing a Trainium2 kernel written in Bass

```python
import jax, jax.numpy as jnp
from jax import lax
import numpy as np

D_MODEL = 1024
BATCH = 1
SEQ = 1024
DEPTH = 2
DEC_BATCH = 8
DEC_SEQ = 1
PAST_LEN = 512
PAGE_SIZE = 128

N_A_LAYERS = DEPTH // 2
N_B_LAYERS = DEPTH - N_A_LAYERS
CHUNK = 128
CM_EXPAND = 2
CM_WIDTH = CM_EXPAND * D_MODEL
CM_GROUPS = 8
CM_GROUP_DIM = CM_WIDTH // CM_GROUPS
FA_HEAD_DIM = 64
FA_HEADS = D_MODEL // FA_HEAD_DIM
FA_WIDTH = FA_HEADS * FA_HEAD_DIM
Q_BLOCK = 128
DEEPNORM_ALPHA = (2.0 * DEPTH) ** 0.25
DEEPNORM_BETA = (8.0 * DEPTH) ** -0.25
FORGET_BIAS_INIT = 2.0
LN_EPS = 1e-5

kernel_name = 'hybrid_gmlp_fox_yoco_step'

def layer_norm(x, g, b):
    xf = x.astype(jnp.float32)
    mu = jnp.mean(xf, axis=-1, keepdims=True)
    var = jnp.mean(jnp.square(xf - mu), axis=-1, keepdims=True)
    y = (xf - mu) * lax.rsqrt(var + LN_EPS) * g.astype(jnp.float32) + b.astype(jnp.float32)
    return y.astype(x.dtype)

def ada_modulation(c, w_ada, b_ada):
    m = (jax.nn.silu(c) @ w_ada + b_ada)[:, None, :]
    return m[..., :D_MODEL], m[..., D_MODEL:2 * D_MODEL], m[..., 2 * D_MODEL:]

def spatial_gate(vn, w_s, b_s):
    rows = vn.shape[1]
    causal = jnp.tril(jnp.ones((rows, rows), dtype=bool))
    w = jnp.where(causal[None], w_s[:, :rows, :rows], 0.0)
    return jnp.einsum('gts,nsgd->ntgd', w, vn) + b_s[:, :rows].T[None, :, :, None]

def chunk_mlp_mixer(h, w_in, b_in, ln_v_g, ln_v_b, w_s, b_s, w_out, b_out):
    n, s, _ = h.shape
    p = h @ w_in + b_in
    u = jax.nn.gelu(p[..., :CM_WIDTH])
    v = jax.nn.gelu(p[..., CM_WIDTH:2 * CM_WIDTH])
    z = p[..., 2 * CM_WIDTH:]
    vn = layer_norm(v, ln_v_g, ln_v_b)
    rows = min(s, CHUNK)
    sg = spatial_gate(vn.reshape(n * (s // rows), rows, CM_GROUPS, CM_GROUP_DIM), w_s, b_s)
    y = (u * sg.reshape(n, s, CM_WIDTH) * jax.nn.silu(z)) @ w_out + b_out
    return y, vn

def shared_kv(xs, kv_w, kv_b):
    n, s, _ = xs.shape
    p = xs @ kv_w + kv_b
    k = p[..., :FA_WIDTH].reshape(n, s, FA_HEADS, FA_HEAD_DIM)
    v = p[..., FA_WIDTH:2 * FA_WIDTH].reshape(n, s, FA_HEADS, FA_HEAD_DIM)
    logf = jax.nn.log_sigmoid(p[..., 2 * FA_WIDTH:].astype(jnp.float32))
    return k, v, logf

def forget_attend(q, c_q, q_pos, k, v, c_k, k_pos):
    logits = jnp.einsum('nqhd,nkhd->nhqk', q, k).astype(jnp.float32) * (FA_HEAD_DIM ** -0.5)
    decay = jnp.swapaxes(c_q, 1, 2)[..., :, None] - jnp.swapaxes(c_k, 1, 2)[..., None, :]
    causal = k_pos[None, :] <= q_pos[:, None]
    logits = jnp.where(causal, logits + decay, -jnp.inf)
    p = jax.nn.softmax(logits, axis=-1)
    return jnp.einsum('nhqk,nkhd->nqhd', p.astype(v.dtype), v)

def forgetting_attention_mixer(h, k, v, c_k, c_q, q_pos, k_pos, w_in, b_in, w_out, b_out):
    n, s, _ = h.shape
    p = h @ w_in + b_in
    q = p[..., :FA_WIDTH].reshape(n, s, FA_HEADS, FA_HEAD_DIM)
    z = p[..., FA_WIDTH:]
    blk = Q_BLOCK if s % Q_BLOCK == 0 else s
    nb = s // blk
    qb = jnp.swapaxes(q.reshape(n, nb, blk, FA_HEADS, FA_HEAD_DIM), 0, 1)
    cb = jnp.swapaxes(c_q.reshape(n, nb, blk, FA_HEADS), 0, 1)
    pb = q_pos.reshape(nb, blk)
    o = lax.map(lambda a: forget_attend(a[0], a[1], a[2], k, v, c_k, k_pos), (qb, cb, pb))
    o = jnp.swapaxes(o, 0, 1).reshape(n, s, FA_WIDTH)
    return (o * jax.nn.silu(z)) @ w_out + b_out

def setup_inputs(seed: int = 0) -> dict:
    key = jax.random.key(seed)
    ks = jax.random.split(key, 32)
    f32 = jnp.float32

    def nrm(k, shape, scale):
        return scale * jax.random.normal(k, shape, f32)

    n_pages = PAST_LEN // PAGE_SIZE
    n_used = DEC_BATCH * n_pages
    n_phys = n_used + n_used // 4
    x_prompt = nrm(ks[0], (BATCH, SEQ, D_MODEL), 1.0)
    x_sample = nrm(ks[1], (DEC_BATCH, DEC_SEQ, D_MODEL), 1.0)
    c_prompt = nrm(ks[2], (BATCH, D_MODEL), 1.0)
    c_sample = nrm(ks[3], (DEC_BATCH, D_MODEL), 1.0)
    cache_k = nrm(ks[4], (n_phys, PAGE_SIZE, FA_HEADS, FA_HEAD_DIM), 1.0)
    cache_v = nrm(ks[5], (n_phys, PAGE_SIZE, FA_HEADS, FA_HEAD_DIM), 1.0)
    cache_logf = jax.nn.log_sigmoid(FORGET_BIAS_INIT + jax.random.normal(ks[6], (n_phys, PAGE_SIZE, FA_HEADS), f32))
    page_table = jax.random.permutation(ks[7], n_phys)[:n_used].reshape(DEC_BATCH, n_pages).astype(jnp.int32)
    w_ada = nrm(ks[8], (DEPTH, D_MODEL, 3 * D_MODEL), 0.1 * D_MODEL ** -0.5)
    b_ada = nrm(ks[9], (DEPTH, 3 * D_MODEL), 0.02)
    ln_g = 1.0 + nrm(ks[10], (DEPTH, D_MODEL), 0.02)
    ln_b = nrm(ks[11], (DEPTH, D_MODEL), 0.02)
    cm_w_in = nrm(ks[12], (N_A_LAYERS, D_MODEL, 3 * CM_WIDTH), D_MODEL ** -0.5)
    cm_b_in = nrm(ks[13], (N_A_LAYERS, 3 * CM_WIDTH), 0.02)
    cm_ln_v_g = 1.0 + nrm(ks[14], (N_A_LAYERS, CM_WIDTH), 0.02)
    cm_ln_v_b = nrm(ks[15], (N_A_LAYERS, CM_WIDTH), 0.02)
    cm_w_s = nrm(ks[16], (N_A_LAYERS, CM_GROUPS, CHUNK, CHUNK), CHUNK ** -0.5)
    cm_b_s = 1.0 + nrm(ks[17], (N_A_LAYERS, CM_GROUPS, CHUNK), 0.02)
    cm_w_out = nrm(ks[18], (N_A_LAYERS, CM_WIDTH, D_MODEL), DEEPNORM_BETA * CM_WIDTH ** -0.5)
    cm_b_out = nrm(ks[19], (N_A_LAYERS, D_MODEL), 0.02)
    kv_w = nrm(ks[20], (D_MODEL, 2 * FA_WIDTH + FA_HEADS), D_MODEL ** -0.5)
    kv_b = nrm(ks[21], (2 * FA_WIDTH + FA_HEADS,), 0.02).at[2 * FA_WIDTH:].add(FORGET_BIAS_INIT)
    fa_w_in = nrm(ks[22], (N_B_LAYERS, D_MODEL, 2 * FA_WIDTH), D_MODEL ** -0.5)
    fa_b_in = nrm(ks[23], (N_B_LAYERS, 2 * FA_WIDTH), 0.02)
    fa_w_out = nrm(ks[24], (N_B_LAYERS, FA_WIDTH, D_MODEL), DEEPNORM_BETA * FA_WIDTH ** -0.5)
    fa_b_out = nrm(ks[25], (N_B_LAYERS, D_MODEL), 0.02)
    return {'x_prompt': x_prompt, 'x_sample': x_sample, 'c_prompt': c_prompt, 'c_sample': c_sample,
            'cache_k': cache_k, 'cache_v': cache_v, 'cache_logf': cache_logf, 'page_table': page_table,
            'w_ada': w_ada, 'b_ada': b_ada, 'ln_g': ln_g, 'ln_b': ln_b,
            'cm_w_in': cm_w_in, 'cm_b_in': cm_b_in, 'cm_ln_v_g': cm_ln_v_g, 'cm_ln_v_b': cm_ln_v_b,
            'cm_w_s': cm_w_s, 'cm_b_s': cm_b_s, 'cm_w_out': cm_w_out, 'cm_b_out': cm_b_out,
            'kv_w': kv_w, 'kv_b': kv_b,
            'fa_w_in': fa_w_in, 'fa_b_in': fa_b_in, 'fa_w_out': fa_w_out, 'fa_b_out': fa_b_out}

def reference(x_prompt, x_sample, c_prompt, c_sample, cache_k, cache_v, cache_logf, page_table,
              w_ada, b_ada, ln_g, ln_b,
              cm_w_in, cm_b_in, cm_ln_v_g, cm_ln_v_b, cm_w_s, cm_b_s, cm_w_out, cm_b_out,
              kv_w, kv_b, fa_w_in, fa_b_in, fa_w_out, fa_b_out):

    def run_trunk(x, c, past):
        n, s, _ = x.shape
        pos0 = 0 if past is None else past[0].shape[1]
        q_pos = pos0 + jnp.arange(s, dtype=jnp.int32)
        k_pos = jnp.arange(pos0 + s, dtype=jnp.int32)
        chunk_rows = []
        new_rows = None
        shared = None
        for layer in range(DEPTH):
            if layer == N_A_LAYERS:
                k_new, v_new, logf_new = shared_kv(x, kv_w, kv_b)
                new_rows = (k_new, v_new, logf_new)
                if past is None:
                    k_all, v_all, logf_all = k_new, v_new, logf_new
                else:
                    k_all = jnp.concatenate([past[0], k_new], axis=1)
                    v_all = jnp.concatenate([past[1], v_new], axis=1)
                    logf_all = jnp.concatenate([past[2].astype(jnp.float32), logf_new], axis=1)
                shared = (k_all, v_all, jnp.cumsum(logf_all, axis=1))
            shift, scale, gate = ada_modulation(c, w_ada[layer], b_ada[layer])
            h = x * (1.0 + scale) + shift
            if layer < N_A_LAYERS:
                f, vn = chunk_mlp_mixer(h, cm_w_in[layer], cm_b_in[layer], cm_ln_v_g[layer], cm_ln_v_b[layer],
                                        cm_w_s[layer], cm_b_s[layer], cm_w_out[layer], cm_b_out[layer])
                chunk_rows.append(vn)
            else:
                j = layer - N_A_LAYERS
                k_all, v_all, c_all = shared
                f = forgetting_attention_mixer(h, k_all, v_all, c_all, c_all[:, pos0:], q_pos, k_pos,
                                               fa_w_in[j], fa_b_in[j], fa_w_out[j], fa_b_out[j])
            x = layer_norm(DEEPNORM_ALPHA * x + (1.0 + gate) * f, ln_g[layer], ln_b[layer])
        return x, new_rows, chunk_rows

    y_prompt, rows_p, _ = run_trunk(x_prompt, c_prompt, None)
    k_prompt, v_prompt, logf_prompt = rows_p

    db = page_table.shape[0]
    k_past = cache_k[page_table].reshape(db, -1, FA_HEADS, FA_HEAD_DIM)
    v_past = cache_v[page_table].reshape(db, -1, FA_HEADS, FA_HEAD_DIM)
    logf_past = cache_logf[page_table].reshape(db, -1, FA_HEADS)
    y_sample, rows_s, chunk_rows_s = run_trunk(x_sample, c_sample, (k_past, v_past, logf_past))
    k_sample, v_sample, logf_sample = rows_s
    chunk_v_sample = jnp.stack(chunk_rows_s)
    return (y_prompt, y_sample, k_prompt, v_prompt, logf_prompt, k_sample, v_sample, logf_sample, chunk_v_sample)


_drawn_inputs = setup_inputs


def setup_inputs(seed=0):
    import zlib

    import numpy as np

    out = dict(_drawn_inputs(seed))
    spreads = {}
    factors = {'cache_logf': 3.112,
     'cm_ln_v_g': 2.754,
     'cm_ln_v_b': 2.75,
     'cm_b_s': 8.0,
     'cm_b_out': 3.965,
     'fa_b_in': 8.0,
     'fa_b_out': 3.978}
    for name, (base, spread) in spreads.items():
        noise = np.random.default_rng([zlib.crc32(name.encode()), seed]).standard_normal(out[name].shape)
        drawn = base * np.exp(spread * noise) if base else spread * noise
        out[name] = __import__('jax').numpy.asarray(drawn.astype(out[name].dtype))
    for name, factor in factors.items():
        out[name] = (out[name] * factor).astype(out[name].dtype)
    return out
```

```python
from contextlib import ExitStack

import concourse.bass as bass
from concourse import mybir

F32 = mybir.dt.float32
F32R = mybir.dt.float32r
BF16 = mybir.dt.bfloat16
I32 = mybir.dt.int32
ACT = mybir.ActivationFunctionType
ALU = mybir.AluOpType
AX = mybir.AxisListType

P = 128
D = 1024
KB = D // P
T = 1024
TT = T // P
NS = 8
TA = T + NS
TH = TA // 3
W = 2 * D
WB = W // P
H = 16
HD = 64
NP = 4
PAST = NP * P
HALF = 512
ALPHA = 4.0 ** 0.25
EPS = 1e-5
SCALE = HD ** -0.5
MASKED = -1e30

U_V, U_ZU, U_OUT, U_F, U_B, U_FA = 0, WB, 3 * WB, 4 * WB, 4 * WB + 1, 4 * WB + 1 + 4 * KB
U_FS = U_FA + KB
N_UNITS = U_FS

COLS = {}
_n = 0
for _name, _k in (("b_ada", 48), ("b_in", 48), ("b_out", 8), ("b_kqvz", 32), ("b_f", 1), ("fa_b_out", 8),
                  ("ln_g", 16), ("ln_b", 16), ("v_g", 16), ("v_b", 16), ("w_s00", 16), ("b_s0", 16)):
    COLS[_name] = (_n, _k)
    _n += _k
N_COLS = _n


def wait(eng, sem, value):
    if isinstance(value, int) and value <= 0:
        return
    eng.wait_ge(sem, value)


def settle(eng, sem):
    eng.sem_inc(sem, 1)


def trunk(nc, units, w_ada, c_t, x_t, cols_d, ws_t, bs_row, ln_rows, table, cache_k, cache_v, cache_f,
          y_out, ys_out, k_out, v_out, f_out, kqv_s_out, vn_out):
    ctx = ExitStack()
    with ctx:
        sems = {}

        def S(name):
            if name not in sems:
                sems[name] = ctx.enter_context(nc.semaphore(name))
            return sems[name]

        BASE = 16512
        R1 = BASE
        R2 = R1 + 2 * KB * TA * 4
        RW = R2 + WB * TA * 4
        R3 = RW + 6 * 4096
        RC = R3 + 45216

        def at(name, shape, dt, offset):
            return nc.alloc_sbuf_tensor_at(name, shape, dt, offset=offset)

        const_end = [RC]

        def const(name, shape, dt=F32):
            n = 1
            for s in shape[1:]:
                n *= s
            t = at(name, shape, dt, const_end[0])
            const_end[0] += (n * (2 if dt == BF16 else 4) + 31) // 32 * 32
            assert const_end[0] <= 229368
            return t

        raw = at("raw", [P, 2, KB, P], F32, RW)
        w_hi = at("w_hi", [P, 2, KB, P], F32R, RW + 8192)
        w_lo = at("w_lo", [P, 2, KB, P], F32R, RW + 16384)

        h_hi = at("h_hi", [P, KB, TA], F32R, R1)
        h_lo = at("h_lo", [P, KB, TA], F32R, R1 + KB * TA * 4)
        xT = at("xT", [P, KB, TA], F32, R1 + KB * TA * 4)
        ada_first = at("ada_first", [P, 16, KB, P], F32, R2)
        V = at("V", [P, WB, TT, P], F32, R2 + 512)
        yT = at("yT", [P, WB, TA], F32, R2)
        y_hi = at("y_hi", [P, WB, TA], F32R, R2)
        y_lo = at("y_lo", [P, WB, TA], F32R, R1)
        Cst = at("Cst", [P, WB, P], F32, R3)
        wsT = at("wsT", [P, KB, P], F32, R3 + 8192)
        vcur = at("vcur", [P, 2, TT, P], F32, R3 + 12288)
        tmp0 = at("tmp0", [P, TA], F32, R3 + 20480)
        tmp1 = at("tmp1", [P, TA], F32, R3 + 24608)
        tmps = [tmp0, tmp1]
        sgm = at("sgm", [P, TT, P], F32, R3 + 28736)
        bs_b = at("bs_b", [P, KB, P], F32, R3 + 28736)
        ada_ring = at("ada_ring", [P, 2, KB, P], F32, R3 + 32832)
        cT = at("cT", [P, KB, 9], F32, R3 + 32832)
        thc = at("thc", [P, KB, 9], F32, R3 + 33344)
        hsf = at("hsf", [P, KB, NS], F32, R3 + 33856)
        vstat = at("vstat", [P, TT, 4, 6], F32, R3 + 34368)
        rT = at("rT", [P, KB, T], F32, R3)
        y_tmp = at("y_tmp", [P, 2, TA], F32R, R3 + 32832)
        xb = at("xb", [P, 2, T], F32, R3 + 32832)
        fg = at("fg", [P, TA], F32, R3 + 41088)
        xhat = at("xhat", [P, 2, KB, P], F32, R1)
        x1f = at("x1f", [P, 2, KB, P], F32, R1 + 8192)
        x_hi = at("x_hi", [P, KB, T], F32R, R2)
        x_lo = at("x_lo", [P, KB, T], F32R, R2 + 32768)
        y2T = at("y2T", [P, KB, T], F32, R1)
        kq_hi = at("kq_hi", [P, 2, 2, T], F32R, R1 + 32768)
        kq_lo = at("kq_lo", [P, 2, 2, T], F32R, R1 + 49152)
        Vhl = at("Vhl", [P, TT, 2, 2, HD], F32R, R3)
        vT = at("vT", [P, T], F32, R3 + 8192)
        kf = at("kf", [P, T], F32, R3 + 12288)
        zth = at("zth", [P, HALF], F32, R3 + 16384)
        zb = at("zb", [P, HALF], F32, R3 + 18432)
        prob = at("prob", [P, T], F32, R3 + 20480)
        pt_hi = at("pt_hi", [P, TT, P], F32R, R3 + 24576)
        pt_lo = at("pt_lo", [P, TT, P], F32R, R3 + 28672)
        ckb = at("ckb", [P, 2, T], F32, R3 + 32768)
        otok = at("otok", [P, TT, P], F32, R3 + 40960)
        fp = at("fp", [H, TA], F32, R3)
        fe = at("fe", [H, TA], F32, R3 + 20480)
        f_ones = at("f_ones", [H, T], F32, R3 + 28672)
        fc = at("fc", [H, T], F32, R3 + 12288)
        y2_hi = at("y2_hi", [P, KB, T], F32R, R1 + 32768)
        y2_lo = at("y2_lo", [P, KB, T], F32R, R2 + 32768)
        r2T = at("r2T", [P, KB, T], F32, R1)
        pages = at("pages", [P, 2, NP, D], F32, R2)
        xb2 = at("xb2", [P, 2, T], F32, R3)
        g_row = at("g_row", [P, D], F32, R3)
        b_row = at("b_row", [P, D], F32, R3 + 4096)
        fg2 = at("fg2", [P, 2, HALF], F32, R3 + 8192)
        xh2 = at("xh2", [P, 2, D], F32, R3 + 12288)
        qtok = at("qtok", [NS, D], F32, R3 + 12288)
        ktok = at("ktok", [NS, D], F32, R3 + 16384)
        yo = at("yo", [P, 2, D], F32, R3 + 20480)
        qb = at("qb", [P, D], F32, R3 + 28672)
        vtok = at("vtok", [NS, D], F32, R3 + 32768)
        scol = at("scol", [P, NP, NS, H], F32, R3 + 36864)
        pTd = at("pTd", [P, NP, P], F32, R3 + 36864)
        fpg = at("fpg", [P, NP, NS, H], F32, R3 + 38912)
        cd = at("cd", [P, PAST + 1], F32, R3 + 40960)
        Ld = at("Ld", [P, PAST + 1], F32, R3 + 43040)
        assert 43040 + 2052 <= 45216

        cols = const("cols", [P, N_COLS])
        ident = const("ident", [P, P])
        identb = const("identb", [P, P], BF16)
        ones = const("ones", [P, P])
        maskb = const("maskb", [P, P], BF16)
        mT = const("mT", [P, 48, 9])
        scT = const("scT", [P, KB, 9])
        one_p = const("one_p", [P, KB])
        xS = const("xS", [P, KB, NS])
        vS = const("vS", [P, WB, NS])
        vnS = const("vnS", [P, WB, NS])
        sq = const("sq", [P, WB, NS])
        sgS = const("sgS", [P, WB, NS])
        rS = const("rS", [P, KB, NS])
        x1S = const("x1S", [P, KB, 9])
        hS = const("hS", [P, KB, 9])
        kqvzS = const("kqvzS", [P, 4, KB, 9])
        red = const("red", [P, NS])
        mean = const("mean", [P, NS])
        rsd = const("rsd", [P, NS])
        mv = const("mv", [P, TT, 2])
        vr = const("vr", [P, TT])
        vnm = const("vnm", [P, TT])
        hbz = const("hbz", [P, WB])
        g1 = const("g1", [P, KB])
        gb = const("gb", [P, KB])
        gS = const("gS", [P, KB, NS])
        lst = const("lst", [P, 2, 6])
        lmv = const("lmv", [P, 2, 2])
        lr = const("lr", [P, 2])
        lnm = const("lnm", [P, 2])
        nmin = const("nmin", [P, 2])
        rsum = const("rsum", [P, 2])
        rcp = const("rcp", [P, 2])
        otmp = const("otmp", [P, HD])
        hbz2 = const("hbz2", [P, 1])
        fS = const("fS", [H, NS])
        mask8 = const("mask8", [NS, NS, H])
        maskp = const("maskp", [P, NS])
        ex = at("ex", [NS, 2, NS, H], F32, R3 + 24576)
        sn = at("sn", [NS, 2, H], F32, R3 + 26112)
        pd = at("pd", [NS, P], F32, R3 + 25600)
        pdx = at("pdx", [P, NS], F32, R3 + 26240)
        dn = const("dn", [P, 4])
        oS = at("oS", [P, KB, NS], F32, R3 + 26368)
        ptab = const("ptab", [1, NS * NP], I32)

        def col(name, i=None):
            a, n = COLS[name]
            return cols[:, a:a + n] if i is None else cols[:, a + i:a + i + 1]

        def col_at(name, i):
            a, _ = COLS[name]
            return cols[:, bass.ds(a + i, 1)] if not isinstance(i, int) else col(name, i)

        def wide(ap, n):
            return ap.rearrange("p (a o) -> p a o", o=1).broadcast_to([ap.shape[0], ap.shape[1], n])

        def over(ap, n):
            return ap.rearrange("p (o b) -> p o b", o=1).broadcast_to([ap.shape[0], n, ap.shape[1]])

        ps = [ctx.enter_context(nc.psum_tensor(f"bank{i}{i + 1}", [P, 2, 512], F32)) for i in (0, 2, 4, 6)]

        def bank(b):
            return ps[b // 2][:, b % 2, :]

        SUMS = {1: 3, 2: 7, 3: 7}

        def pair(n):
            return ps[n][:, :, :].rearrange("p a b -> p (a b)")

        def third(s, t):
            return bank(3 * s + t)[:, 0:TH]

        def thirds(eng_op, s, sb, *rest):
            for t in range(3):
                last = eng_op(t, third(s, t), sb[:, t * TH:(t + 1) * TH], *rest)
            return last

        scr_x = nc.dram_tensor("scr_x", [KB, P, T], F32, kind="Internal").ap()
        scr_c = nc.dram_tensor("scr_c", [H, T], F32, kind="Internal").ap()
        scr_q = nc.dram_tensor("scr_q", [NS, D], F32, kind="Internal").ap()

        block = ctx.enter_context(nc.Block())

        @block.sync
        def _(sp):
            sp.dma_start(cT[:, :, :], c_t).then_inc(S("c_in"), 16)
            sp.dma_start(cols[:, :], cols_d).then_inc(S("cols_in"), 16)
            for a in (8, 0):
                for i in range(4):
                    sp.dma_start(ada_first[:, a + 2 * i:a + 2 * i + 2, :, :],
                                 w_ada[a + 2 * i:a + 2 * i + 2, :, :, :].rearrange("u p k c -> p u k c"))\
                      .then_inc(S(f"ada_in{(a + 2 * i) // 4}"), 16)
            sp.dma_start(xT[:, :, :], x_t).then_inc(S("x_in"), 16)
            sp.dma_start(wsT[:, :, :], ws_t).then_inc(S("ws_in"), 16)
            sp.dma_start(bs_b[:, :, :], bs_row.broadcast_to([P, KB, P])).then_inc(S("bs_in"), 16)
            sp.dma_start(ptab[:, :], table).then_inc(S("table_in"), 16)

            def load(u, slot, i=None):
                wait(sp, S("lo_ready"), u - 1)
                sp.dma_start(raw[:, slot, :, :], units[u, :, :, :]).then_inc(S(f"raw_in{slot}"), 16)

            load(0, 0)
            load(1, 1)
            with sp.Fori(0, WB // 2 - 1) as i:
                for s in range(2):
                    load(2 * i + 2 + s, s)
            for j in range(1):
                for s in range(2):
                    load(U_ZU + s, s)
                for s in range(2):
                    if s == 0:
                        sp.wait_ge(S("v_norm"), 1)
                    sp.dma_start(ada_ring[:, s, :, :], w_ada[16 + s, :, :, :]).then_inc(S(f"ada_ring_in{s}"), 16)
            with sp.Fori(1, WB) as j:
                for s in range(2):
                    load(U_ZU + 2 * j + s, s)
                for s in range(2):
                    sp.wait_ge(S("ada_used"), 2 * j - 1 + s)
                    sp.dma_start(ada_ring[:, s, :, :], w_ada[16 + 2 * j + s, :, :, :])\
                      .then_inc(S(f"ada_ring_in{s}"), 16)
            for b in range(KB):
                for s in range(2):
                    load(U_OUT + 2 * b + s, s)
                if b == 0:
                    sp.wait_ge(S("y_split"), WB)
                if b >= 2:
                    sp.wait_ge(S("r_ready"), b - 1)
                sp.dma_start(xb[:, b % 2, :], x_t[:, b, 0:T]).then_inc(S(f"xb_in{b % 2}"), 16)
            load(U_F, 0)

            def load_b(m, s):
                wait(sp, S("mm"), 3 * m - 5)
                if isinstance(m, int) and m == 1:
                    sp.wait_ge(S("f_mm"), 1)
                settle(sp, S("settled"))
                load(U_B + m, s)

            for m in range(4):
                load_b(m, (m + 1) % 2)
            with sp.Fori(1, KB) as j:
                for q in range(4):
                    load_b(4 * j + q, (q + 1) % 2)
            for b in range(KB):
                if b == 0:
                    sp.wait_ge(S("mm"), 12 * KB - 5)
                if b == 1:
                    sp.wait_ge(S("mm"), 12 * KB - 2)
                load(U_FA + b, (U_FA + b) % 2)
                if b == 0:
                    sp.wait_ge(S("v_hl"), KB)
                    sp.wait_ge(S("pv_done"), 16 * KB)
                if b >= 2:
                    sp.wait_ge(S("r2_ready"), 2 * b - 2)
                sp.wait_ge(S("scr_x_out0"), 16 * TT // 2)
                sp.wait_ge(S("scr_x_out1"), 16 * TT // 2)
                sp.dma_start(xb2[:, b % 2, :], scr_x[b, :, :]).then_inc(S(f"xb2_in{b % 2}"), 16)
            sp.wait_ge(S("r2_ready"), 2 * KB)
            sp.dma_start(g_row[:, :], ln_rows[0:1, :].broadcast_to([P, D])).then_inc(S("rows_in"), 16)
            sp.dma_start(b_row[:, :], ln_rows[1:2, :].broadcast_to([P, D])).then_inc(S("rows_in"), 16)
            sp.wait_ge(S("tok_ready"), 1)
            sp.dma_start(scr_q, qtok[:, :]).then_inc(S("scr_q"), 16)
            sp.wait_ge(S("scr_q"), 16)
            for b in range(NS):
                if b == 0:
                    sp.wait_ge(S("pv_done"), 16 * KB)
                wait(sp, S("qk_prod"), b)
                sp.dma_start(qb[:, :], scr_q[b:b + 1, :].broadcast_to([P, D])).then_inc(S("qb_in"), 16)
            for b in range(KB):
                u = U_FS + b
                wait(sp, S("lo_ready"), U_FS)
                wait(sp, S("fs_used"), b - 1)
                sp.dma_start(raw[:, u % 2, :, :], units[U_FA + b, :, :, :]).then_inc(S(f"raw_in{u % 2}"), 16)
            for t in range(TT):
                sp.wait_ge(S("yo_ready"), t + 1)
                sp.dma_start(y_out[t * P:(t + 1) * P, :], yo[:, t % 2, :]).then_inc(S(f"y_out{t % 2}"), 16)
            sp.wait_ge(S("y_out0"), 16 * TT // 2)
            sp.wait_ge(S("y_out1"), 16 * TT // 2)
            sp.wait_ge(S("ys_ready"), 1)
            sp.dma_start(ys_out, rS[:, :, :]).then_inc(S("ys_out"), 16)
            sp.wait_ge(S("ys_out"), 16)

        @block.gpsimd
        def _(pool):
            g = nc.gpsimd
            g.memset(ident[:, :], 1.0).then_inc(S("pc"), 1)
            g.memset(ones[:, :], 1.0).then_inc(S("pc"), 1)
            g.memset(maskb[:, :], MASKED).then_inc(S("pc"), 1)
            g.memset(identb[:, :], 1.0).then_inc(S("pc"), 1)
            g.memset(mask8[:, :, :], 1.0).then_inc(S("pc"), 1)
            g.memset(maskp[:, :], 1.0).then_inc(S("pc"), 1)
            pool.wait_ge(S("pc"), 6)
            for m in (ident, identb):
                g.affine_select(out=m[:, :], in_=m[:, :], compare_op=ALU.is_equal, fill=0.0, base=0,
                                pattern=[[-1, P]], channel_multiplier=1).then_inc(S("consts"), 1)
            g.affine_select(out=maskb[:, :], in_=maskb[:, :], compare_op=ALU.is_gt, fill=0.0, base=0,
                            pattern=[[1, P]], channel_multiplier=-1).then_inc(S("consts"), 1)
            g.affine_select(out=mask8[:, :, :], in_=mask8[:, :, :], compare_op=ALU.is_equal, fill=0.0, base=0,
                            pattern=[[1, NS], [0, H]], channel_multiplier=-1).then_inc(S("consts"), 1)
            g.affine_select(out=maskp[:, :], in_=maskp[:, :], compare_op=ALU.is_ge, fill=0.0, base=0,
                            pattern=[[-H, NS]], channel_multiplier=1).then_inc(S("pc"), 1)
            pool.wait_ge(S("pc"), 7)
            g.affine_select(out=maskp[:, :], in_=maskp[:, :], compare_op=ALU.is_ge, fill=0.0, base=H - 1,
                            pattern=[[H, NS]], channel_multiplier=-1).then_inc(S("consts"), 1)
            pool.wait_ge(S("ws_in"), 16)
            g.affine_select(out=wsT[:, :, :], in_=wsT[:, :, :], compare_op=ALU.is_ge, fill=0.0, base=0,
                            pattern=[[0, KB], [1, P]], channel_multiplier=-1).then_inc(S("ws_ready"), 1)
            def norm_v(j, s):
                wait(pool, S("spatial_done"), j - 1)
                pool.wait_ge(S("v_norm"), 1)
                g.tensor_tensor(vcur[:, s, :, :], V[:, j, :, :], wide(vr[:, :], P), ALU.mult).then_inc(S("vcur_mul"), 1)
                pool.wait_ge(S("vcur_mul"), j + 1)
                g.tensor_tensor(vcur[:, s, :, :], vcur[:, s, :, :], wide(vnm[:, :], P), ALU.add)\
                    .then_inc(S("vcur_ready"), 1)

            pool.wait_ge(S("v_norm"), 1)
            norm_v(0, 0)
            norm_v(1, 1)
            with pool.Fori(1, WB // 2) as i:
                for s in range(2):
                    norm_v(2 * i + s, s)
            pool.wait_ge(S("vn_s"), 1)
            pool.dma_start(vn_out, vnS[:, :, :]).then_inc(S("vn_out"), 16)
            for t in range(TT):
                pool.wait_ge(S("x1f_ready"), t + 1)
                pool.dma_start(scr_x[:, :, t * P:(t + 1) * P].rearrange("k p t -> p k t"), x1f[:, t % 2, :, :])\
                    .then_inc(S(f"scr_x_out{t % 2}"), 16)
            pool.wait_ge(S("f_ready"), 1)
            pool.dma_start(f_out, fp[:, :]).then_inc(S("f_out"), 16)
            pool.wait_ge(S("c_ready"), 1)
            pool.dma_start(scr_c, fc[:, :]).then_inc(S("scr_c"), 16)
            pool.wait_ge(S("scr_c"), 16)

            def load_c(j, h):
                pool.dma_start(ckb[:, h, :], scr_c[bass.ds(2 * j + h, 1), :].broadcast_to([P, T])
                               if not isinstance(j, int) else scr_c[2 * j + h:2 * j + h + 1, :].broadcast_to([P, T]))\
                    .then_inc(S(f"ckb_in{h}"), 16)

            def store_kv(j, par):
                pool.wait_ge(S("evac"), 12 * j + 3)
                wait(pool, S("k_out"), 16 * j)
                g.tensor_tensor(kf[:, :], kq_hi[:, par, 0, :].bitcast(F32), kq_lo[:, par, 0, :].bitcast(F32), ALU.add)\
                    .then_inc(S("kf_ready"), 1)
                pool.wait_ge(S("kf_ready"), j + 1)
                pool.dma_start(k_out[j, :, :], kf[:, :]).then_inc(S("k_out"), 16)
                pool.wait_ge(S("evac"), 12 * j + 9)
                settle(pool, S("settled"))
                pool.dma_start(v_out[j, :, :], vT[:, :]).then_inc(S("v_out"), 16)

            pool.wait_ge(S("f_out"), 16)
            load_c(0, 0)
            load_c(0, 1)
            store_kv(0, 0)

            def phase(j, par):
                store_kv(j + 1, 1 - par)
                for h in range(2):
                    pool.wait_ge(S("nl_ready"), 16 * j + 15 + h)
                    load_c(j + 1, h)

            phase(0, 0)
            with pool.Fori(0, KB // 2 - 1) as i2:
                phase(2 * i2 + 1, 1)
                phase(2 * i2 + 2, 0)
            pool.wait_ge(S("evac"), 12 * KB)
            pool.dma_start(kqv_s_out, kqvzS[:, 0:3, :, :]).then_inc(S("kqv_s_out"), 16)

            pool.wait_ge(S("table_in"), 16)
            pool.wait_ge(S("lo_ready"), U_B + 4 * KB)
            pool.wait_ge(S("mm"), 12 * KB)
            pool.wait_ge(S("pv_done"), 16 * KB)
            pool.wait_ge(S("o_evac"), 16 * KB)
            with pool.Fori(0, NS) as b:
                for p in range(NP):
                    page = pool.value_load(ptab[0:1, bass.ds(b * NP + p, 1)], min_val=0, max_val=cache_f.shape[0] - 1)
                    pool.dma_start(fpg[:, p, b, :], cache_f[bass.ds(page, 1), :, :].rearrange("a p h -> p (a h)"))\
                        .then_inc(S("fpg_in"), 16)

            def load_pages(cache, b, s, n):
                wait(pool, S("pages_used"), n - 1)
                for p in range(NP):
                    page = pool.value_load(ptab[0:1, bass.ds(b * NP + p, 1)], min_val=0, max_val=cache_k.shape[0] - 1)
                    pool.dma_start(pages[:, s, p, :], cache[bass.ds(page, 1), :, :].rearrange("a p c -> p (a c)"))\
                        .then_inc(S(f"pages_in{s}"), 16)

            for cache, n0 in ((cache_k, 0), (cache_v, NS)):
                first = 2 if n0 == 0 else 0
                for b in range(first):
                    load_pages(cache, b, b % 2, n0 + b)
                with pool.Fori(first // 2, NS // 2) as i:
                    for s in range(2):
                        load_pages(cache, 2 * i + s, s, n0 + 2 * i + s)
            for name, n in (("vn_out", 16), ("k_out", 16 * KB), ("v_out", 16 * KB), ("kqv_s_out", 16)):
                pool.wait_ge(S(name), n)

        @block.scalar
        def _(act):
            A = nc.scalar.activation

            def hi(u, slot, n, free="hl_used", value=None):
                act.wait_ge(S(f"raw_in{slot}"), 16 * n)
                wait(act, S(free), u - 1 if value is None else value)
                A(w_hi[:, slot, :, :], raw[:, slot, :, :], ACT.Copy).then_inc(S("hi_ready"), 1)

            def hi_scaled(u, slot, n, free, value):
                act.wait_ge(S(f"raw_in{slot}"), 16 * n)
                wait(act, S(free), value)
                for k in range(KB):
                    last = A(w_hi[:, slot, k, :], raw[:, slot, k, :], ACT.Copy, scale=one_p[:, k:k + 1])
                last.then_inc(S("hi_ready"), 1)

            act.wait_ge(S("c_in"), 16)
            A(thc[:, :, :], cT[:, :, :], ACT.Tanh, scale=0.5).then_inc(S("thc"), 1)
            act.wait_ge(S("hs_ready"), 1)
            A(h_hi[:, :, T:TA], hsf[:, :, :], ACT.Copy).then_inc(S("hs_hi"), 1)
            hi(0, 0, 1)
            for k in range(KB):
                act.wait_ge(S("hf_ready"), k + 1)
                A(h_hi[:, k, 0:T], tmps[k % 2][:, 0:T], ACT.Copy).then_inc(S("h_hi_ready"), 1)

            def gelu_v(j, s):
                act.wait_ge(S("hl_used"), U_V + j + 1)
                wait(act, S("v_tr"), j - 1)
                wait(act, S("v_s"), j - 1)
                for t in range(3):
                    last = A(tmps[s][:, t * TH:(t + 1) * TH], third(s, t), ACT.Gelu_apprx_tanh,
                             bias=col_at("b_in", WB + j))
                last.then_inc(S("v_act"), 1)

            act.wait_ge(S("h_ready"), KB)
            for j in range(2):
                hi(j + 1, (j + 1) % 2, (j + 1) // 2 + 1)
                gelu_v(j, j % 2)
            with act.Fori(1, WB // 2) as i:
                for s in range(2):
                    hi(2 * i + s + 1, 1 - s, i + 1 + s)
                    gelu_v(2 * i + s, s)
            act.wait_ge(S("v_var"), 1)
            A(vr[:, :], vr[:, :], ACT.Sqrt).then_inc(S("v_sqrt"), 1)

            def sqrt_s(n):
                act.wait_ge(S("s_var"), n)
                A(rsd[:, :], rsd[:, :], ACT.Sqrt).then_inc(S("s_sqrt"), 1)

            sqrt_s(1)

            def act_zu(j):
                hi(U_ZU + 2 * j + 1, 1, WB // 2 + j + 1)
                act.wait_ge(S("hl_used"), U_ZU + 2 * j + 1)
                wait(act, S("y_ready"), j)
                for t in range(3):
                    last = A(tmp0[:, t * TH:(t + 1) * TH], third(0, t), ACT.Tanh, bias=hbz[:, bass.ds(j, 1)], scale=0.5)
                last.then_inc(S("z_th"), 1)
                hi(U_ZU + 2 * j + 2, 0, WB // 2 + j + 2)
                act.wait_ge(S("ada_used"), 2 * j + 2)
                for t in range(3):
                    last = A(tmp1[:, t * TH:(t + 1) * TH], third(1, t), ACT.Gelu_apprx_tanh, bias=col_at("b_in", j))
                last.then_inc(S("u_act"), 1)

            act.wait_ge(S("v_tr"), WB)
            act.wait_ge(S("v_s"), WB)
            act_zu(0)
            with act.Fori(1, WB) as j:
                act_zu(j)

            for k in range(WB):
                if k == 0:
                    act.wait_ge(S("y_ready"), WB)
                    act.wait_ge(S("ada_used"), 2 * WB)
                wait(act, S("y_lo_ready"), k - 1)
                A(y_tmp[:, k % 2, :], yT[:, k, :], ACT.Copy).then_inc(S("y_tmp_ready"), 1)
            for b in range(KB):
                for s in range(2):
                    u = U_OUT + 2 * b + s + 1
                    hi(u, u % 2, u // 2 + 1)
                if b == 0:
                    act.wait_ge(S("gate_ready"), 1)
                act.wait_ge(S("hl_used"), U_OUT + 2 * b + 2)
                wait(act, S("r_ready"), b)
                for t in range(3):
                    last = A(fg[:, t * TH:(t + 1) * TH], third(b % 2, t), ACT.Identity,
                             bias=gb[:, b:b + 1], scale=g1[:, b:b + 1])
                last.then_inc(S("fg_ready"), 1)

            def layer_norm_act(t, n0, dst, free):
                act.wait_ge(S("ln_var"), n0 + t + 1)
                A(lr[:, t % 2:t % 2 + 1], lr[:, t % 2:t % 2 + 1], ACT.Sqrt).then_inc(S("ln_sqrt"), 1)
                act.wait_ge(S("ln_stat"), n0 + t + 1)
                wait(act, S(free), t - 1)
                A(dst, pair(t % 2), ACT.Identity, bias=lnm[:, t % 2:t % 2 + 1], scale=lr[:, t % 2:t % 2 + 1])\
                    .then_inc(S("ln_hat"), 1)

            def x1_hi(t):
                act.wait_ge(S("x1f_ready"), t + 1)
                if t == 0:
                    act.wait_ge(S("hl_used"), U_OUT + 2 * KB)
                A(x_hi[:, :, t * P:(t + 1) * P], x1f[:, t % 2, :, :], ACT.Copy).then_inc(S("x1_hi"), 1)

            sqrt_s(2)
            for t in range(TT):
                layer_norm_act(t, 0, xhat[:, t % 2, :, :].rearrange("p a b -> p (a b)"), "ln1_back")
                if t >= 1:
                    x1_hi(t - 1)
            x1_hi(TT - 1)

            act.wait_ge(S("f_abs"), 1)
            A(fe[:, :], fe[:, :], ACT.Exp, scale=-1.0).then_inc(S("f_exp"), 1)
            act.wait_ge(S("f_exp"), 1)
            A(fe[:, :], fe[:, :], ACT.Ln, bias=1.0).then_inc(S("f_ln"), 1)

            def split_hi(j, q):
                u = U_B + 4 * j + q
                n = 2 * j + (U_B + q) // 2 + 1
                free = ("hl_used", u - 1) if isinstance(j, int) and 4 * j + q < 2 else ("mm", 12 * j + 3 * q - 3)
                (hi_scaled if q in (1, 3) else hi)(u, (U_B + q) % 2, n, *free)

            def evac_hi(j, q, half, par):
                act.wait_ge(S("mm"), 12 * j + 3 * q + half + 2)
                src = bank((q + half + 1) % 2)
                cs = slice(half * HALF, half * HALF + HALF)
                if q == 0:
                    wait(act, S("s_done"), 16 * j - 16)
                    wait(act, S("kf_ready"), j - 1)
                    settle(act, S("settled"))
                    A(kq_hi[:, par, 0, cs], src, ACT.Identity, bias=col_at("b_kqvz", j)).then_inc(S("ev_hi"), 1)
                elif q == 1:
                    act.wait_ge(S("evac"), 12 * j + 4)
                    settle(act, S("settled"))
                    A(kq_hi[:, par, 1, cs], src, ACT.Identity, bias=kqvzS[:, 1, j, 8:9]).then_inc(S("ev_hi"), 1)
                elif q == 3:
                    if half == 0:
                        act.wait_ge(S("hbz_ready"), j + 1)
                    wait(act, S("zs_done"), 2 * j + half)
                    A(zth[:, :], src, ACT.Tanh, bias=hbz2[:, 0:1], scale=0.5).then_inc(S("ev_hi"), 1)

            def v_hi(j):
                act.wait_ge(S("vt_done"), j + 1)
                wait(act, S("pv_done"), 16 * j)
                A(Vhl[:, :, :, 0, :], pair(2).rearrange("p (t h d) -> p t h d", t=TT, h=2), ACT.Copy)\
                    .then_inc(S("v_hi"), 1)

            def pt_high(j, i):
                nk = i // 2 + 1
                act.wait_ge(S("t_done"), 16 * j + i + 1)
                wait(act, S("pv_done"), 16 * j + i)
                A(pt_hi[:, 0:nk, :], pair(2)[:, 0:nk * P], ACT.Copy).then_inc(S("pt_hi"), 1)

            def exp(j, i):
                nk = i // 2 + 1
                act.wait_ge(S("nl_ready"), 16 * j + i + 1)
                wait(act, S("rcp_ready"), 16 * j + max(i - 1, 0))
                A(prob[:, 0:nk * P], prob[:, 0:nk * P], ACT.Exp, bias=nmin[:, i % 2:i % 2 + 1], scale=-1.0,
                  accum_out=rsum[:, i % 2:i % 2 + 1]).then_inc(S("p_ready"), 1)

            def o_part(j, i):
                act.wait_ge(S("pv_done"), 16 * j + i + 1)
                act.wait_ge(S("rcp_ready"), 16 * j + i + 1)
                wait(act, S("o_evac"), 16 * j + i)
                A(otmp[:, :], bank(6 + i % 2)[:, HD:2 * HD], ACT.Copy, scale=rcp[:, i % 2:i % 2 + 1])\
                    .then_inc(S("otmp_ready"), 1)

            split_hi(0, 0)
            for q in range(4):
                split_hi((q + 1) // 4, (q + 1) % 4)
                if q != 2:
                    for half in range(2):
                        evac_hi(0, q, half, 0)
            act.wait_ge(S("f_out"), 16)
            v_hi(0)

            HALVES = {2: (0, 0), 5: (0, 1), 7: (1, 0), 10: (1, 1), 13: (2, 0), 15: (2, 1)}

            def phase(j, par, more):
                for i in range(16):
                    if i >= 1:
                        pt_high(j, i - 1)
                    exp(j, i)
                    if more and i in HALVES and HALVES[i][0] != 2:
                        evac_hi(j + 1, *HALVES[i], 1 - par)
                    if more and i in (0, 5, 10):
                        split_hi(j + 1, i // 5 + 1)
                    if i >= 1:
                        o_part(j, i - 1)
                pt_high(j, 15)
                o_part(j, 15)
                if more:
                    split_hi(j + 2, 0)
                    evac_hi(j + 1, 3, 0, 1 - par)
                    v_hi(j + 1)
                    evac_hi(j + 1, 3, 1, 1 - par)

            phase(0, 0, True)
            with act.Fori(0, KB // 2 - 1) as i2:
                phase(2 * i2 + 1, 1, True)
                phase(2 * i2 + 2, 0, True)
            phase(KB - 1, 1, False)

            act.wait_ge(S("y2_ready"), KB)
            act.wait_ge(S("s_done"), 16 * KB)
            act.wait_ge(S("kf_ready"), KB)
            for k in range(KB):
                A(y2_hi[:, k, :], y2T[:, k, :], ACT.Copy).then_inc(S("y2_hi"), 1)
            for b in range(KB):
                if b + 1 < KB:
                    u = U_FA + b + 1
                    hi(u, u % 2, u // 2 + 1, *(("fa_mm", 2 * b) if b else ("mm", 12 * KB)))
                for half in range(2):
                    n = 2 * b + half
                    if n == 0:
                        act.wait_ge(S("v_out"), 16 * KB)
                    act.wait_ge(S("fa_mm"), n + 1)
                    wait(act, S("r2_ready"), n - 1)
                    A(fg2[:, half, :], bank(half), ACT.Identity, bias=gb[:, b:b + 1], scale=g1[:, b:b + 1])\
                        .then_inc(S("fg2_ready"), 1)
            act.wait_ge(S("d_max"), 1)
            A(Ld[:, :], Ld[:, :], ACT.Exp, bias=dn[:, 0:1], accum_out=dn[:, 1:2]).then_inc(S("d_exp"), 1)
            A(sq[:, 0:KB, :], kqvzS[:, 3, :, 0:NS], ACT.Tanh, scale=0.5).then_inc(S("zs_th"), 1)
            sqrt_s(3)

            for t in range(TT):
                if t == 0:
                    act.wait_ge(S("sn_ready"), 1)
                    act.wait_ge(S("scr_q"), 16)
                layer_norm_act(t, TT, xh2[:, t % 2, :], "yo_ready")

        @block.vector
        def _(dve):
            v = nc.vector
            chain = [0]

            def link(ins):
                chain[0] += 1
                ins.then_inc(S("dve_chain"), 1)
                dve.wait_ge(S("dve_chain"), chain[0])

            def lo(u, slot):
                dve.wait_ge(S("hi_ready"), u + 1)
                v.tensor_tensor(w_lo[:, slot, :, :], raw[:, slot, :, :], w_hi[:, slot, :, :].bitcast(F32), ALU.subtract)\
                    .then_inc(S("lo_ready"), 1)

            def lo_scaled(u, slot):
                dve.wait_ge(S("hi_ready"), u + 1)
                for k in range(KB):
                    last = v.scalar_tensor_tensor(w_lo[:, slot, k, :], raw[:, slot, k, :], one_p[:, k:k + 1],
                                                  w_hi[:, slot, k, :].bitcast(F32), ALU.mult, ALU.subtract)
                last.then_inc(S("lo_ready"), 1)

            dve.wait_ge(S("c_in"), 16)
            dve.wait_ge(S("thc"), 1)
            link(v.scalar_tensor_tensor(scT[:, :, :], thc[:, :, :], 1.0, cT[:, :, :], ALU.add, ALU.mult))
            v.tensor_scalar(scT[:, :, :], scT[:, :, :], 0.5, None, ALU.mult).then_inc(S("sc_ready"), 1)
            dve.wait_ge(S("cols_in"), 16)
            v.tensor_scalar(hbz[:, :], cols[:, COLS["b_in"][0] + 2 * WB:COLS["b_in"][0] + 3 * WB], 0.5, None, ALU.mult)\
                .then_inc(S("hbz"), 1)
            dve.wait_ge(S("ada0_mm"), 1)
            link(v.tensor_tensor(mT[:, 0:16, :], bank(0)[:, 0:16 * 9].rearrange("p (a n) -> p a n", n=9),
                                 wide(cols[:, 0:16], 9), ALU.add))
            link(v.tensor_scalar(one_p[:, :], mT[:, 8:16, 8], 1.0, None, ALU.add))
            dve.wait_ge(S("x_in"), 16)
            v.tensor_copy(xS[:, :, :], xT[:, :, T:TA])
            link(v.tensor_scalar(hsf[:, :, :], mT[:, 8:16, 0:NS], 1.0, None, ALU.add))
            link(v.tensor_tensor(hsf[:, :, :], hsf[:, :, :], xT[:, :, T:TA], ALU.mult))
            v.tensor_tensor(hsf[:, :, :], hsf[:, :, :], mT[:, 0:8, 0:NS], ALU.add).then_inc(S("hs_ready"), 1)
            dve.wait_ge(S("hs_hi"), 1)
            v.tensor_tensor(h_lo[:, :, T:TA], hsf[:, :, :], h_hi[:, :, T:TA].bitcast(F32), ALU.subtract)
            lo(0, 0)

            def h_low(k):
                dve.wait_ge(S("h_hi_ready"), k + 1)
                v.tensor_tensor(h_lo[:, k, 0:T], tmps[k % 2][:, 0:T], h_hi[:, k, 0:T].bitcast(F32), ALU.subtract)\
                    .then_inc(S("h_ready"), 1)

            for k in range(KB):
                wait(dve, S("h_ready"), k - 1)
                v.tensor_scalar(tmps[k % 2][:, 0:T], xT[:, k, 0:T], one_p[:, k:k + 1], mT[:, k, 8:9], ALU.mult, ALU.add)\
                    .then_inc(S("hf_ready"), 1)
                if k >= 1:
                    h_low(k - 1)
            h_low(KB - 1)
            dve.wait_ge(S("rs_mm"), 1)
            dve.wait_ge(S("bs_in"), 16)
            for j in range(WB):
                g = j // 2
                last = v.scalar_tensor_tensor(Cst[:, j, :], pair(3)[:, g * P:(g + 1) * P], col("v_b", j),
                                              bs_b[:, g, :], ALU.mult, ALU.add)
            last.then_inc(S("cst_ready"), 1)

            def store_v(j, s):
                dve.wait_ge(S("v_act"), j + 1)
                v.tensor_copy(vS[:, j, :], tmps[s][:, T:TA]).then_inc(S("v_s"), 1)
                dve.wait_ge(S("v_tr"), j + 1)
                v.tensor_copy(V[:, j, :, :], pair(3).rearrange("p (t c) -> p t c", c=P)).then_inc(S("v_stored"), 1)

            def stats(jq):
                dve.wait_ge(S("v_stored"), 4 * jq + 4)
                for t in range(TT):
                    last = v.bn_stats(vstat[:, t, jq, :], V[:, 4 * jq:4 * jq + 4, t, :])
                return last

            for j in range(WB):
                lo(j + 1, (j + 1) % 2)
                store_v(j, j % 2)
                if j % 4 == 3:
                    last = stats(j // 4)
            link(last)
            for t in range(TT):
                last = v.bn_aggr(mv[:, t, :], vstat[:, t, :, :].rearrange("p a b -> p (a b)"))
            link(last)
            v.tensor_scalar(vr[:, :], mv[:, :, 1], EPS, None, ALU.add).then_inc(S("v_var"), 1)
            dve.wait_ge(S("v_sqrt"), 1)
            link(v.reciprocal(vr[:, :], vr[:, :]))
            v.scalar_tensor_tensor(vnm[:, :], mv[:, :, 0], -1.0, vr[:, :], ALU.mult, ALU.mult).then_inc(S("v_norm"), 1)

            def sample_norm(n, x, nb, gname, g0, bname, out):
                link(v.tensor_reduce(red[:, :], x.rearrange("p b n -> p n b"), AX.X, ALU.add))
                v.tensor_scalar(red[:, :], red[:, :], 1.0 / (nb * P), None, ALU.mult).then_inc(S("s_sum"), 1)
                dve.wait_ge(S("s_mm"), 2 * n - 1)
                link(v.tensor_copy(mean[:, :], bank(SUMS[n])[:, 0:NS]))
                link(v.tensor_tensor(out, x, over(mean[:, :], nb), ALU.subtract))
                link(v.tensor_tensor(sq[:, 0:nb, :], out, out, ALU.mult))
                link(v.tensor_reduce(red[:, :], sq[:, 0:nb, :].rearrange("p b n -> p n b"), AX.X, ALU.add))
                v.tensor_scalar(red[:, :], red[:, :], 1.0 / (nb * P), None, ALU.mult).then_inc(S("s_sum"), 1)
                dve.wait_ge(S("s_mm"), 2 * n)
                v.tensor_scalar(rsd[:, :], bank(SUMS[n])[:, 0:NS], EPS, None, ALU.add).then_inc(S("s_var"), 1)
                dve.wait_ge(S("s_sqrt"), n)
                link(v.reciprocal(rsd[:, :], rsd[:, :]))
                link(v.tensor_tensor(out, out, over(rsd[:, :], nb), ALU.mult))
                a, b = COLS[gname][0] + g0, COLS[bname][0] + g0
                link(v.tensor_tensor(out, out, wide(cols[:, a:a + nb], NS), ALU.mult))
                return v.tensor_tensor(out, out, wide(cols[:, b:b + nb], NS), ALU.add)

            link(sample_norm(1, vS[:, :, :], WB, "v_g", 0, "v_b", vnS[:, :, :]))
            link(v.tensor_tensor(sgS[:, :, :], vnS[:, :, :], wide(col("w_s00"), NS), ALU.mult))
            v.tensor_tensor(sgS[:, :, :], sgS[:, :, :], wide(col("b_s0"), NS), ALU.add).then_inc(S("vn_s"), 1)

            def dve_zu(j):
                lo(U_ZU + 2 * j + 1, 1)
                dve.wait_ge(S("z_th"), j + 1)
                v.tensor_scalar(tmp0[:, :], tmp0[:, :], 1.0, None, ALU.add).then_inc(S("z_th1"), 1)
                dve.wait_ge(S("z_th1"), j + 1)
                for t in range(3):
                    last = v.scalar_tensor_tensor(tmp0[:, t * TH:(t + 1) * TH], third(0, t), col_at("b_in", 2 * WB + j),
                                                  tmp0[:, t * TH:(t + 1) * TH], ALU.add, ALU.mult)
                last.then_inc(S("z_silu"), 1)
                dve.wait_ge(S("spatial_done"), j + 1)
                wait(dve, S("y_ready"), j)
                v.scalar_tensor_tensor(sgm[:, :, :], pair(3).rearrange("p (t c) -> p t c", c=P), col_at("v_g", j),
                                       Cst[:, bass.ds(j, 1), :].broadcast_to([P, TT, P]), ALU.mult, ALU.add)\
                    .then_inc(S("sgm_ready"), 1)
                lo(U_ZU + 2 * j + 2, 0)
                dve.wait_ge(S("u_act"), j + 1)
                dve.wait_ge(S("z_silu"), j + 1)
                v.tensor_tensor(tmp0[:, :], tmp0[:, :], tmp1[:, :], ALU.mult).then_inc(S("uz_ready"), 1)
                v.tensor_tensor(mT[:, bass.ds(16 + 2 * j, 2), :], bank(5)[:, 360:378].rearrange("p (a n) -> p a n", n=9),
                                cols[:, bass.ds(16 + 2 * j, 2)].rearrange("p (a o) -> p a o", o=1).broadcast_to([P, 2, 9]),
                                ALU.add).then_inc(S("ada_ev"), 1)
                dve.wait_ge(S("uz_ready"), j + 1)
                dve.wait_ge(S("sgm_ready"), j + 1)
                v.scalar_tensor_tensor(yT[:, j, T:TA], tmp0[:, T:TA], 0.5, sgS[:, j, :], ALU.mult, ALU.mult)
                v.scalar_tensor_tensor(yT[:, j, 0:T], tmp0[:, 0:T], 0.5, sgm[:, :, :].rearrange("p t c -> p (t c)"),
                                       ALU.mult, ALU.mult).then_inc(S("y_ready"), 1)

            dve.wait_ge(S("cst_ready"), 1)
            dve.wait_ge(S("vn_s"), 1)
            dve_zu(0)
            with dve.Fori(1, WB) as j:
                dve_zu(j)

            for k in range(WB):
                dve.wait_ge(S("y_tmp_ready"), k + 1)
                if k == 0:
                    dve.wait_ge(S("hl_used"), U_OUT)
                v.tensor_tensor(y_lo[:, k, :], yT[:, k, :], y_tmp[:, k % 2, :].bitcast(F32), ALU.subtract)\
                    .then_inc(S("y_lo_ready"), 1)
                dve.wait_ge(S("y_lo_ready"), k + 1)
                v.tensor_copy(y_hi[:, k, :], yT[:, k, :]).then_inc(S("y_split"), 1)

            def gates(layer, bname):
                a = 24 * layer + 16
                link(v.tensor_scalar(g1[:, :], mT[:, a:a + 8, 8], 1.0, None, ALU.add))
                v.tensor_scalar(gS[:, :, :], mT[:, a:a + 8, 0:NS], 1.0, None, ALU.add)
                link(v.tensor_tensor(gb[:, :], g1[:, :], col(bname), ALU.mult))

            dve.wait_ge(S("ada_ev"), WB)
            gates(0, "b_out")
            v.tensor_scalar(one_p[:, :], mT[:, 32:40, 8], 1.0, None, ALU.add).then_inc(S("gate_ready"), 1)
            for b in range(KB):
                for s in range(2):
                    u = U_OUT + 2 * b + s + 1
                    lo(u, u % 2)
                dve.wait_ge(S("fg_ready"), b + 1)
                dve.wait_ge(S(f"xb_in{b % 2}"), 16 * (b // 2 + 1))
                v.tensor_scalar(rS[:, b, :], bank(3 * (b % 2) + 2)[:, TH - NS:TH], col("b_out", b), None, ALU.add)
                v.scalar_tensor_tensor(rT[:, b, :], xb[:, b % 2, :], ALPHA, fg[:, 0:T], ALU.mult, ALU.add)\
                    .then_inc(S("r_ready"), 1)

            dve.wait_ge(S("r_ready"), KB)

            def residual_s(x):
                link(v.tensor_tensor(rS[:, :, :], rS[:, :, :], gS[:, :, :], ALU.mult))
                link(v.scalar_tensor_tensor(rS[:, :, :], x, ALPHA, rS[:, :, :], ALU.mult, ALU.add))

            residual_s(xS[:, :, :])
            link(sample_norm(2, rS[:, :, :], KB, "ln_g", 0, "ln_b", x1S[:, :, 0:NS]))
            v.tensor_copy(x1S[:, :, 8], mT[:, 24:32, 8])
            v.tensor_copy(hS[:, :, 8], mT[:, 24:32, 8])
            link(v.tensor_scalar(hS[:, :, 0:NS], mT[:, 32:40, 0:NS], 1.0, None, ALU.add))
            link(v.tensor_tensor(hS[:, :, 0:NS], hS[:, :, 0:NS], x1S[:, :, 0:NS], ALU.mult))
            v.tensor_tensor(hS[:, :, 0:NS], hS[:, :, 0:NS], mT[:, 24:32, 0:NS], ALU.add).then_inc(S("s_in"), 1)

            def layer_norm_stats(t, n0):
                dve.wait_ge(S("ln_tr"), n0 + t + 1)
                for h in range(2):
                    last = v.bn_stats(lst[:, h, :], ps[t % 2][:, h, :])
                link(last)
                wait(dve, S("ln_hat"), n0 + t - 1)
                link(v.bn_aggr(lmv[:, t % 2, :], lst[:, :, :].rearrange("p a b -> p (a b)")))
                v.tensor_scalar(lr[:, t % 2:t % 2 + 1], lmv[:, t % 2, 1:2], EPS, None, ALU.add)\
                    .then_inc(S("ln_var"), 1)
                dve.wait_ge(S("ln_sqrt"), n0 + t + 1)
                link(v.reciprocal(lr[:, t % 2:t % 2 + 1], lr[:, t % 2:t % 2 + 1]))
                v.scalar_tensor_tensor(lnm[:, t % 2:t % 2 + 1], lmv[:, t % 2, 0:1], -1.0, lr[:, t % 2:t % 2 + 1],
                                       ALU.mult, ALU.mult).then_inc(S("ln_stat"), 1)

            def x1_back(t):
                dve.wait_ge(S("ln1_back"), t + 1)
                if t >= 2:
                    dve.wait_ge(S(f"scr_x_out{t % 2}"), 16 * (t // 2))
                    dve.wait_ge(S("x1_hi"), t - 1)
                    dve.wait_ge(S("x1_ready"), t - 1)
                for k in range(KB):
                    last = v.tensor_scalar(x1f[:, t % 2, k, :], pair(2 + t % 2)[:, k * P:(k + 1) * P],
                                           col("ln_g", k), col("ln_b", k), ALU.mult, ALU.add)
                last.then_inc(S("x1f_ready"), 1)

            def x1_lo(t):
                dve.wait_ge(S("x1_hi"), t + 1)
                v.tensor_tensor(x_lo[:, :, t * P:(t + 1) * P], x1f[:, t % 2, :, :],
                                x_hi[:, :, t * P:(t + 1) * P].bitcast(F32), ALU.subtract).then_inc(S("x1_ready"), 1)

            for t in range(TT):
                layer_norm_stats(t, 0)
                if t >= 1:
                    x1_back(t - 1)
                if t >= 2:
                    x1_lo(t - 2)
            x1_back(TT - 1)
            x1_lo(TT - 2)
            x1_lo(TT - 1)

            dve.wait_ge(S("f_mm"), 1)
            for half in range(2):
                v.tensor_scalar(fp[:, half * HALF:(half + 1) * HALF], bank(half)[0:H, :], cols[0:H, COLS["b_f"][0]:COLS["b_f"][0] + 1],
                                None, ALU.add)
            link(v.tensor_scalar(fp[:, T:TA], bank(2)[0:H, 0:NS], cols[0:H, COLS["b_f"][0]:COLS["b_f"][0] + 1], None, ALU.add))
            v.tensor_scalar(fe[:, :], fp[:, :], -1.0, None, ALU.mult).then_inc(S("f_neg"), 1)
            dve.wait_ge(S("f_neg"), 1)
            v.tensor_tensor(fe[:, :], fe[:, :], fp[:, :], ALU.max).then_inc(S("f_abs"), 1)
            v.memset(f_ones[:, :], 1.0)
            dve.wait_ge(S("f_ln"), 1)
            v.scalar_tensor_tensor(fp[:, :], fp[:, :], 0.0, fe[:, :], ALU.min, ALU.subtract).then_inc(S("f_ready"), 1)
            dve.wait_ge(S("f_ready"), 1)
            v.tensor_copy(fS[:, :], fp[:, T:TA])
            link(v.tensor_tensor_scan(fc[:, :], f_ones[:, :], fp[:, 0:T], 0.0, ALU.mult, ALU.add))
            v.tensor_scalar(fc[:, :], fc[:, :], -1.0 / SCALE, None, ALU.mult).then_inc(S("c_ready"), 1)

            def split_lo(j, q):
                (lo_scaled if q in (1, 3) else lo)(U_B + 4 * j + q, (U_B + q) % 2)

            def evac_s(j, q):
                dve.wait_ge(S("mm"), 12 * j + 3 * q + 1)
                v.tensor_scalar(kqvzS[:, q, j, :], bank(q % 2)[:, 0:9], col_at("b_kqvz", q * KB + j), None, ALU.add)\
                    .then_inc(S("evac"), 1)
                if q == 3:
                    dve.wait_ge(S("evac"), 12 * j + 3 * q + 1)
                    wait(dve, S("ev_hi"), 6 * j)
                    v.tensor_scalar(hbz2[:, :], kqvzS[:, 3, j, 8:9], 0.5, None, ALU.mult).then_inc(S("hbz_ready"), 1)

            EV = {0: 0, 1: 2, 3: 4}

            def evac_lo(j, q, half, par):
                src = bank((q + half + 1) % 2)
                cs = slice(half * HALF, half * HALF + HALF)
                if q == 2:
                    dve.wait_ge(S("mm"), 12 * j + 3 * q + half + 2)
                    wait(dve, S("v_out"), 16 * j)
                    wait(dve, S("vt_done"), j)
                    v.tensor_scalar(vT[:, cs], src, col_at("b_kqvz", 2 * KB + j), None, ALU.add).then_inc(S("evac"), 1)
                    return
                dve.wait_ge(S("ev_hi"), 6 * j + EV[q] + half + 1)
                if q == 0:
                    v.scalar_tensor_tensor(kq_lo[:, par, 0, cs], src, col_at("b_kqvz", j),
                                           kq_hi[:, par, 0, cs].bitcast(F32), ALU.add, ALU.subtract).then_inc(S("evac"), 1)
                elif q == 1:
                    v.scalar_tensor_tensor(kq_lo[:, par, 1, cs], src, kqvzS[:, 1, j, 8:9],
                                           kq_hi[:, par, 1, cs].bitcast(F32), ALU.add, ALU.subtract).then_inc(S("evac"), 1)
                else:
                    wait(dve, S("zs_done"), 2 * j + half)
                    if isinstance(j, int) and j == 0:
                        for t in range(2):
                            dve.wait_ge(S(f"scr_x_out{t}"), 16 * TT // 2)
                    v.tensor_scalar(zb[:, :], src, kqvzS[:, 3, j, 8:9], 0.5, ALU.add, ALU.mult).then_inc(S("evac"), 1)
                    dve.wait_ge(S("evac"), 12 * j + 3 * q + half + 2)
                    v.scalar_tensor_tensor(y2T[:, j, cs], zth[:, :], 1.0, zb[:, :], ALU.add, ALU.mult)\
                        .then_inc(S("zs_done"), 1)

            def v_lo(j):
                dve.wait_ge(S("v_hi"), j + 1)
                v.tensor_tensor(Vhl[:, :, :, 1, :], pair(2).rearrange("p (t h d) -> p t h d", t=TT, h=2),
                                Vhl[:, :, :, 0, :].bitcast(F32), ALU.subtract).then_inc(S("v_hl"), 1)

            def logits(j, i):
                nk = i // 2 + 1
                dve.wait_ge(S("s_done"), 16 * j + i + 1)
                if i < 2:
                    dve.wait_ge(S(f"ckb_in{i}"), 16 * j + 16)
                wait(dve, S("t_done"), 16 * j + i)
                settle(dve, S("settled"))
                v.tensor_tensor_reduce(out=prob[:, 0:nk * P], in0=pair(1)[:, 0:nk * P], in1=ckb[:, i % 2, 0:nk * P],
                                       scale=-SCALE, scalar=3e38, op0=ALU.add, op1=ALU.min,
                                       accum_out=nmin[:, i % 2:i % 2 + 1]).then_inc(S("nl_ready"), 1)

            def pt_low(j, i):
                nk = i // 2 + 1
                dve.wait_ge(S("pt_hi"), 16 * j + i + 1)
                v.tensor_tensor(pt_lo[:, 0:nk, :], pair(2)[:, 0:nk * P].rearrange("p (t c) -> p t c", c=P),
                                pt_hi[:, 0:nk, :].bitcast(F32), ALU.subtract).then_inc(S("pt_ready"), 1)
                dve.wait_ge(S("p_ready"), 16 * j + i + 1)
                wait(dve, S("otmp_ready"), 16 * j + max(i - 1, 0))
                v.reciprocal(rcp[:, i % 2:i % 2 + 1], rsum[:, i % 2:i % 2 + 1]).then_inc(S("rcp_ready"), 1)

            def o_full(j, i):
                dve.wait_ge(S("otmp_ready"), 16 * j + i + 1)
                if i == 0:
                    wait(dve, S("ot_done"), j)
                v.scalar_tensor_tensor(otok[:, i // 2, (i % 2) * HD:(i % 2 + 1) * HD], bank(6 + i % 2)[:, 0:HD],
                                       rcp[:, i % 2:i % 2 + 1], otmp[:, :], ALU.mult, ALU.add).then_inc(S("o_evac"), 1)

            def gate_o(j):
                dve.wait_ge(S("ot_done"), j + 1)
                dve.wait_ge(S("zs_done"), 2 * j + 2)
                v.tensor_tensor(y2T[:, j, :], pair(1), y2T[:, j, :], ALU.mult).then_inc(S("y2_ready"), 1)

            split_lo(0, 0)
            for q in range(4):
                split_lo((q + 1) // 4, (q + 1) % 4)
                evac_s(0, q)
                for half in range(2):
                    evac_lo(0, q, half, 0)
            v_lo(0)

            HALVES = {2: (0, 0), 5: (0, 1), 7: (1, 0), 10: (1, 1), 13: (2, 0), 15: (2, 1)}

            def phase(j, par, more):
                for i in range(16):
                    logits(j, i)
                    if i >= 1:
                        pt_low(j, i - 1)
                    if more and i == 0:
                        evac_s(j + 1, 0)
                    if more and i in HALVES:
                        evac_lo(j + 1, *HALVES[i], 1 - par)
                    if more and i in (5, 10):
                        evac_s(j + 1, i // 5)
                    if more and i in (0, 5, 10):
                        split_lo(j + 1, i // 5 + 1)
                    if i >= 1:
                        o_full(j, i - 1)
                pt_low(j, 15)
                o_full(j, 15)
                if more:
                    evac_s(j + 1, 3)
                    split_lo(j + 2, 0)
                    evac_lo(j + 1, 3, 0, 1 - par)
                    v_lo(j + 1)
                gate_o(j)
                if more:
                    evac_lo(j + 1, 3, 1, 1 - par)

            phase(0, 0, True)
            with dve.Fori(0, KB // 2 - 1) as i2:
                phase(2 * i2 + 1, 1, True)
                phase(2 * i2 + 2, 0, True)
            phase(KB - 1, 1, False)

            gates(1, "fa_b_out")
            for k in range(KB):
                dve.wait_ge(S("y2_hi"), k + 1)
                v.tensor_tensor(y2_lo[:, k, :], y2T[:, k, :], y2_hi[:, k, :].bitcast(F32), ALU.subtract)\
                    .then_inc(S("y2_split"), 1)
            for b in range(KB):
                if b + 1 < KB:
                    lo(U_FA + b + 1, (U_FA + b + 1) % 2)
                for half in range(2):
                    n = 2 * b + half
                    dve.wait_ge(S("fg2_ready"), n + 1)
                    if half == 0:
                        dve.wait_ge(S(f"xb2_in{b % 2}"), 16 * (b // 2 + 1))
                    v.scalar_tensor_tensor(r2T[:, b, half * HALF:(half + 1) * HALF], xb2[:, b % 2, half * HALF:(half + 1) * HALF],
                                           ALPHA, fg2[:, half, :], ALU.mult, ALU.add).then_inc(S("r2_ready"), 1)

            dve.wait_ge(S("k_out"), 16 * KB)
            for n, (q, dst) in enumerate(((1, qtok), (0, ktok), (2, vtok))):
                dve.wait_ge(S("tok_mm"), n + 1)
                v.tensor_copy(dst[:, :], pair(n % 2 + 2)[0:NS, :]).then_inc(S("tok_ready"), 1)
            dve.wait_ge(S("tok_ready"), 3)
            link(v.tensor_tensor(yo[0:NS, 0, :], qtok[:, :], ktok[:, :], ALU.mult))
            link(v.tensor_reduce(sn[:, 0, :], yo[0:NS, 0, :].rearrange("p (h d) -> p h d", d=HD), AX.X, ALU.add))
            dve.wait_ge(S("fs_mm"), 1)
            link(v.tensor_copy(sn[:, 1, :], bank(2)[0:NS, 0:H]))
            for c in range(2):
                last = v.tensor_tensor(ex[:, c, :, :], over(sn[:, c, :], NS), mask8[:, :, :], ALU.mult)
            last.then_inc(S("sn_ready"), 1)
            for b in range(NS):
                s = b % 2
                dve.wait_ge(S(f"pages_in{s}"), 16 * NP * (b // 2 + 1))
                dve.wait_ge(S("qb_in"), 16 * (b + 1))
                for p in range(NP):
                    last = v.tensor_tensor(pages[:, s, p, :], pages[:, s, p, :], qb[:, :], ALU.mult)
                last.then_inc(S("qk_prod"), 1)
                dve.wait_ge(S("qk_prod"), b + 1)
                for p in range(NP):
                    last = v.tensor_reduce(scol[:, p, b, :], pages[:, s, p, :].rearrange("p (h d) -> p h d", d=HD), AX.X, ALU.add)
                last.then_inc(S("pages_used"), 1)
            dve.wait_ge(S("d_tr"), 1)
            v.tensor_copy(Ld[:, 0:PAST], bank(4))
            dve.wait_ge(S("d_new"), 1)
            link(v.tensor_copy(dn[:, 2:4], bank(3)[:, 0:2]))
            link(v.tensor_copy(Ld[:, PAST:PAST + 1], dn[:, 3:4]))
            link(v.tensor_tensor_scan(cd[:, :], ones[:, 0:1].broadcast_to([P, PAST + 1]), Ld[:, :], 0.0, ALU.mult, ALU.add))
            dve.wait_ge(S("d_tr"), 2)
            v.scalar_tensor_tensor(Ld[:, PAST:PAST + 1], dn[:, 2:3], SCALE, cd[:, PAST:PAST + 1], ALU.mult, ALU.subtract)
            link(v.scalar_tensor_tensor(Ld[:, 0:PAST], bank(5), SCALE, cd[:, 0:PAST], ALU.mult, ALU.subtract))
            v.tensor_reduce(dn[:, 0:1], Ld[:, :], AX.X, ALU.max, negate=True).then_inc(S("d_max"), 1)
            dve.wait_ge(S("d_exp"), 1)
            link(v.reciprocal(dn[:, 1:2], dn[:, 1:2]))
            link(v.tensor_scalar(Ld[:, :], Ld[:, :], dn[:, 1:2], None, ALU.mult))
            v.tensor_scalar(pdx[:, :], maskp[:, :], Ld[:, PAST:PAST + 1], None, ALU.mult).then_inc(S("d_p"), 1)
            dve.wait_ge(S("d_tr"), 3)
            v.tensor_copy(pTd[:, :, :], bank(4).rearrange("p (a b) -> p a b", b=P))
            v.tensor_copy(pd[:, :], bank(5)[0:NS, 0:P]).then_inc(S("d_pt"), 1)
            dve.wait_ge(S("pages_used"), 2 * NS)
            o4 = bank(6)[:, 0:2 * KB * NS].rearrange("p (b c e) -> p c b e", b=NS, c=KB)
            dve.wait_ge(S("zs_th"), 1)
            for e in range(2):
                v.tensor_copy(oS[e * HD:(e + 1) * HD, :, :], o4[e * HD:(e + 1) * HD, :, :, e])
            link(v.scalar_tensor_tensor(sq[:, 0:KB, :], sq[:, 0:KB, :], 1.0, kqvzS[:, 3, :, 0:NS], ALU.add, ALU.mult))
            v.scalar_tensor_tensor(oS[:, :, :], oS[:, :, :], 0.5, sq[:, 0:KB, :], ALU.mult, ALU.mult).then_inc(S("os_ready"), 1)
            dve.wait_ge(S("fs_used"), KB)
            link(v.tensor_tensor(rS[:, :, :], bank(7)[:, 0:KB * NS].rearrange("p (a b) -> p a b", b=NS),
                                 wide(col("fa_b_out"), NS), ALU.add))
            residual_s(x1S[:, :, 0:NS])
            sample_norm(3, rS[:, :, :], KB, "ln_g", KB, "ln_b", rS[:, :, :]).then_inc(S("ys_ready"), 1)

            dve.wait_ge(S("rows_in"), 32)

            def finish(t):
                dve.wait_ge(S("ln_hat"), TT + t + 1)
                v.tensor_tensor(xh2[:, t % 2, :], xh2[:, t % 2, :], g_row[:, :], ALU.mult).then_inc(S("ln2_mul"), 1)
                dve.wait_ge(S("ln2_mul"), t + 1)
                if t >= 2:
                    dve.wait_ge(S(f"y_out{t % 2}"), 16 * (t // 2))
                v.tensor_tensor(yo[:, t % 2, :], xh2[:, t % 2, :], b_row[:, :], ALU.add).then_inc(S("yo_ready"), 1)

            for t in range(TT):
                layer_norm_stats(t, TT)
                if t >= 1:
                    finish(t - 1)
            finish(TT - 1)

        @block.tensor
        def _(pe):
            mm = nc.tensor.matmul

            def three(out, lhs_hi, lhs_lo, rhs_hi, rhs_lo, first, last):
                mm(out, lhs_lo, rhs_hi, start=first, stop=False)
                mm(out, lhs_hi, rhs_lo, start=False, stop=False)
                return mm(out, lhs_hi, rhs_hi, start=False, stop=last)

            pe.wait_ge(S("sc_ready"), 1)
            for a in (*range(8, 16), *range(8)):
                if a % 4 == 0:
                    pe.wait_ge(S(f"ada_in{a // 4}"), 32)
                for k in range(KB):
                    last = mm(bank(0)[:, a * 9:a * 9 + 9], ada_first[:, a, k, :], scT[:, k, :],
                              start=(k == 0), stop=(k == KB - 1))
            last.then_inc(S("ada0_mm"), 1)
            pe.wait_ge(S("ws_ready"), 1)
            for h in range(2):
                last = mm(ps[3][:, h, :], ones[:, :], wsT[:, 4 * h:4 * h + 4, :], start=True, stop=True)
            last.then_inc(S("rs_mm"), 1)

            def block_a(u, slot, s, k0=0, rhs=(h_hi, h_lo), nk=KB, waits=None):
                pe.wait_ge(S("lo_ready"), u + 1)
                for k in range(KB):
                    if waits:
                        pe.wait_ge(S(waits), k0 + k + 1)
                    for t in range(3):
                        last = three(third(s, t), w_hi[:, slot, k, :], w_lo[:, slot, k, :],
                                     rhs[0][:, k0 + k, t * TH:(t + 1) * TH], rhs[1][:, k0 + k, t * TH:(t + 1) * TH],
                                     k0 + k == 0, k0 + k == nk - 1)
                return last

            def transpose_v(j, s):
                pe.wait_ge(S("v_act"), j + 1)
                wait(pe, S("v_stored"), j)
                for t in range(TT):
                    last = nc.tensor.transpose(pair(3)[:, t * P:(t + 1) * P], tmps[s][:, t * P:(t + 1) * P], ident[:, :])
                last.then_inc(S("v_tr"), 1)

            pe.wait_ge(S("consts"), 5)
            pe.wait_ge(S("h_ready"), KB)
            pe.wait_ge(S("cst_ready"), 1)

            def block_v(j, s):
                wait(pe, S("v_act"), j - 1)
                last = block_a(j, s, s)
                last.then_inc(S("hl_used"), 1)

            block_v(0, 0)
            block_v(1, 1)
            transpose_v(0, 0)
            with pe.Fori(1, WB // 2) as i:
                for s in range(2):
                    block_v(2 * i + s, s)
                    transpose_v(2 * i + s - 1, 1 - s)
            transpose_v(WB - 1, 1)

            def sample_sums(n):
                for i in range(2):
                    pe.wait_ge(S("s_sum"), 2 * n - 1 + i)
                    mm(bank(SUMS[n])[:, 0:NS], ones[:, :], red[:, :], start=True, stop=True).then_inc(S("s_mm"), 1)

            sample_sums(1)

            def block_zu(j, s):
                wait(pe, S("z_silu"), j) if not isinstance(j, int) or j else pe.wait_ge(S("v_act"), WB)
                last = block_a(U_ZU + 2 * j, 0, 0)
                last.then_inc(S("hl_used"), 1)
                pe.wait_ge(S("vcur_ready"), j + 1)
                wait(pe, S("sgm_ready"), j) if not isinstance(j, int) or j else pe.wait_ge(S("v_stored"), WB)
                g = j // 2 if isinstance(j, int) else None
                for t in range(TT):
                    rhs = wsT[:, g, :] if g is not None else wsT[:, bass.ds(block_zu.g, 1), :].rearrange("p a c -> p (a c)")
                    last = mm(pair(3)[:, t * P:(t + 1) * P], vcur[:, s, t, :], rhs, start=True, stop=True)
                last.then_inc(S("spatial_done"), 1)
                if not isinstance(j, int) or j:
                    wait(pe, S("u_act"), j)
                    wait(pe, S("ada_ev"), j)
                else:
                    pe.wait_ge(S("s_var"), 1)
                block_a(U_ZU + 2 * j + 1, 1, 1).then_inc(S("hl_used"), 1)
                for a in range(2):
                    pe.wait_ge(S(f"ada_ring_in{a}"), 16 * (j + 1))
                    for k in range(KB):
                        last = mm(bank(5)[:, 360 + 9 * a:369 + 9 * a], ada_ring[:, a, k, :], scT[:, k, :],
                                  start=(k == 0), stop=(k == KB - 1))
                    last.then_inc(S("ada_used"), 1)

            block_zu(0, 0)
            block_zu(1, 1)
            with pe.Fori(1, WB // 2) as i:
                block_zu.g = i
                for s in range(2):
                    block_zu(2 * i + s, s)

            def block_out(b, s, waits=None):
                if b < 2:
                    pe.wait_ge(S("z_silu" if b == 0 else "ada_ev"), WB)
                    if b == 1:
                        pe.wait_ge(S("u_act"), WB)
                else:
                    pe.wait_ge(S("r_ready"), b - 1)
                block_a(U_OUT + 2 * b, 0, s, 0, (y_hi, y_lo), WB, waits).then_inc(S("hl_used"), 1)
                last = block_a(U_OUT + 2 * b + 1, 1, s, KB, (y_hi, y_lo), WB, waits)
                last.then_inc(S("hl_used"), 1)

            for b in range(KB):
                block_out(b, b % 2, "y_split" if b == 0 else None)

            pe.wait_ge(S("r_ready"), KB)
            sample_sums(2)
            def ln_forward(t, src, n0):
                wait(pe, S("ln_hat"), n0 + t - 1)
                for k in range(KB):
                    last = nc.tensor.transpose(pair(t % 2)[:, k * P:(k + 1) * P], src[:, k, t * P:(t + 1) * P], ident[:, :])
                last.then_inc(S("ln_tr"), 1)

            def ln_backward(t):
                pe.wait_ge(S("ln_hat"), t + 1)
                wait(pe, S("x1f_ready"), t - 1)
                if t == 1:
                    pe.wait_ge(S("s_var"), 2)
                for k in range(KB):
                    last = nc.tensor.transpose(pair(2 + t % 2)[:, k * P:(k + 1) * P], xhat[:, t % 2, k, :], ident[:, :])
                last.then_inc(S("ln1_back"), 1)

            ln_forward(0, rT, 0)
            ln_forward(1, rT, 0)
            for t in range(TT):
                ln_backward(t)
                if t + 2 < TT:
                    ln_forward(t + 2, rT, 0)

            def sample_cols(out, slot, src):
                for k in range(KB):
                    last = mm(out, raw[:, slot, k, :], src[:, k, :], start=(k == 0), stop=(k == KB - 1))
                return last

            def token_step(out, slot, half, k):
                cs = slice(half * HALF, half * HALF + HALF)
                return three(out, w_hi[:, slot, k, :], w_lo[:, slot, k, :], x_hi[:, k, cs], x_lo[:, k, cs],
                             k == 0, k == KB - 1)

            pe.wait_ge(S("lo_ready"), U_F + 1)
            pe.wait_ge(S("s_in"), 1)
            pe.wait_ge(S("x1_ready"), TT)
            for half in range(2):
                for k in range(KB):
                    last = token_step(bank(half), 0, half, k)
            last.then_inc(S("hl_used"), 1)
            sample_cols(bank(2)[:, 0:9], 0, x1S).then_inc(S("f_mm"), 1)

            def step(j, q, n):
                slot = (U_B + q) % 2
                half, k = divmod(n, KB)
                if n == 0:
                    wait(pe, S("evac"), 12 * j + 3 * q - 1)
                    pe.wait_ge(S("lo_ready"), U_B + 4 * j + q + 1)
                    last = sample_cols(bank(q % 2)[:, 0:9], slot, hS if q in (1, 3) else x1S)
                    last.then_inc(S("mm"), 1)
                if k == 0:
                    wait(pe, S("evac"), 12 * j + 3 * q + half)
                last = token_step(bank((q + half + 1) % 2), slot, half, k)
                if k == KB - 1:
                    last.then_inc(S("mm"), 1)

            def transpose_vt(j):
                pe.wait_ge(S("evac"), 12 * j + 9)
                wait(pe, S("pt_ready"), 16 * j)
                for t in range(TT):
                    last = nc.tensor.transpose(pair(2)[:, t * P:(t + 1) * P], vT[:, t * P:(t + 1) * P], ident[:, :])
                last.then_inc(S("vt_done"), 1)

            def scores(j, i, par):
                qt, h = divmod(i, 2)
                nk = qt + 1
                rows = slice(h * HD, (h + 1) * HD)
                qs = slice(qt * P, (qt + 1) * P)
                if i == 0:
                    pe.wait_ge(S("evac"), 12 * j + 6)
                    wait(pe, S("y2_ready"), j)
                wait(pe, S("nl_ready"), 16 * j + i)
                for c in range((nk + 3) // 4):
                    n = min(4, nk - 4 * c) * P
                    ks = slice(c * 512, c * 512 + n)
                    out = ps[1][:, c, 0:n]
                    end = c == (nk - 1) // 4
                    mm(out, kq_lo[rows, par, 1, qs], kq_hi[rows, par, 0, ks], start=True, stop=False)
                    mm(out, kq_hi[rows, par, 1, qs], kq_lo[rows, par, 0, ks], start=False, stop=False)
                    mm(out, kq_hi[rows, par, 1, qs], kq_hi[rows, par, 0, ks], start=False, stop=not end)
                mm(pair(1)[:, qt * P:(qt + 1) * P], identb[:, :], maskb[:, :], start=False, stop=True)\
                    .then_inc(S("s_done"), 1)

            def transpose_p(j, i):
                nk = i // 2 + 1
                pe.wait_ge(S("p_ready"), 16 * j + i + 1)
                wait(pe, S("pt_ready"), 16 * j + i)
                if i == 0:
                    pe.wait_ge(S("v_hl"), j + 1)
                for k in range(nk):
                    last = nc.tensor.transpose(pair(2)[:, k * P:(k + 1) * P], prob[:, k * P:(k + 1) * P], ident[:, :])
                last.then_inc(S("t_done"), 1)

            def values(j, i):
                nk = i // 2 + 1
                h = i % 2
                pe.wait_ge(S("pt_ready"), 16 * j + i + 1)
                wait(pe, S("o_evac"), 16 * j + max(i - 1, 0))
                out = bank(6 + h)
                for k in range(nk):
                    mm(out[:, 0:2 * HD], pt_hi[:, k, :], Vhl[:, k, h, :, :].rearrange("p a d -> p (a d)"),
                       start=(k == 0), stop=False)
                    last = mm(out[:, 0:HD], pt_lo[:, k, :], Vhl[:, k, h, 0, :], start=False, stop=(k == nk - 1))
                last.then_inc(S("pv_done"), 1)

            for q in range(4):
                for n in range(16):
                    if q == 0 and n == 0:
                        pe.wait_ge(S("f_ready"), 1)
                    step(0, q, n)
            transpose_vt(0)

            def phase(j, par, more):
                for i in range(16):
                    if i >= 1:
                        transpose_p(j, i - 1)
                    scores(j, i, par)
                    if more:
                        for n in range(3 * i, 3 * i + 3):
                            step(j + 1, n // 16, n % 16)
                    if i >= 1:
                        values(j, i - 1)

                def z_steps(a, b):
                    for n in range(a, b):
                        if more:
                            step(j + 1, 3, n)

                transpose_p(j, 15)
                z_steps(0, 4)
                values(j, 15)
                z_steps(4, 8)
                if more:
                    transpose_vt(j + 1)
                z_steps(8, 12)
                pe.wait_ge(S("o_evac"), 16 * j + 16)
                for t in range(TT):
                    last = nc.tensor.transpose(pair(1)[:, t * P:(t + 1) * P], otok[:, t, :], ident[:, :])
                last.then_inc(S("ot_done"), 1)
                z_steps(12, 16)

            phase(0, 0, True)
            with pe.Fori(0, KB // 2 - 1) as i2:
                phase(2 * i2 + 1, 1, True)
                phase(2 * i2 + 2, 0, True)
            phase(KB - 1, 1, False)

            for b in range(KB):
                slot = (U_FA + b) % 2
                pe.wait_ge(S("lo_ready"), U_FA + b + 1)
                for half in range(2):
                    cs = slice(half * HALF, half * HALF + HALF)
                    if b == 0:
                        pe.wait_ge(S("evac"), 12 * KB)
                    wait(pe, S("fg2_ready"), 2 * b + half - 1)
                    for k in range(KB):
                        if b == 0 and half == 0:
                            pe.wait_ge(S("y2_split"), k + 1)
                        last = three(bank(half), w_hi[:, slot, k, :], w_lo[:, slot, k, :],
                                     y2_hi[:, k, cs], y2_lo[:, k, cs], k == 0, k == KB - 1)
                    last.then_inc(S("fa_mm"), 1)

            for n, q in enumerate((1, 0, 2)):
                wait(pe, S("tok_ready"), n - 1)
                for c in range(KB):
                    last = mm(pair(n % 2 + 2)[0:NS, c * P:(c + 1) * P], kqvzS[:, q, c, 0:NS], ident[:, :],
                              start=True, stop=True)
                last.then_inc(S("tok_mm"), 1)
            mm(bank(2)[0:NS, 0:H], fS[:, :], ident[0:H, 0:H], start=True, stop=True).then_inc(S("fs_mm"), 1)
            pe.wait_ge(S("tok_ready"), 3)
            pe.wait_ge(S("fpg_in"), 16 * NP * NS)
            for p in range(NP):
                last = nc.tensor.transpose(bank(4)[:, p * P:(p + 1) * P], fpg[:, p, :, :].rearrange("p b h -> p (b h)"), ident[:, :])
            last.then_inc(S("d_tr"), 1)
            pe.wait_ge(S("sn_ready"), 1)
            for c in range(2):
                last = mm(bank(3)[:, c:c + 1], ex[:, c, :, :].rearrange("p b h -> p (b h)"), ones[0:NS, 0:1],
                          start=True, stop=True)
            last.then_inc(S("d_new"), 1)
            pe.wait_ge(S("pages_used"), NS)
            for p in range(NP):
                last = nc.tensor.transpose(bank(5)[:, p * P:(p + 1) * P], scol[:, p, :, :].rearrange("p b h -> p (b h)"), ident[:, :])
            last.then_inc(S("d_tr"), 1)
            pe.wait_ge(S("d_p"), 1)
            for p in range(NP):
                nc.tensor.transpose(bank(4)[:, p * P:(p + 1) * P], Ld[:, p * P:(p + 1) * P], ident[:, :])
            mm(bank(5)[0:NS, 0:P], pdx[:, :], ident[:, :], start=True, stop=True).then_inc(S("d_tr"), 1)
            pe.wait_ge(S("d_pt"), 1)
            for b in range(NS):
                s = b % 2
                pe.wait_ge(S(f"pages_in{s}"), 16 * NP * (NS // 2 + b // 2 + 1))
                for c in range(KB):
                    out = bank(6)[:, (b * KB + c) * 2:(b * KB + c) * 2 + 2]
                    hc = b * H + 2 * c
                    for p in range(NP):
                        mm(out, pages[:, s, p, c * P:(c + 1) * P], pTd[:, p, hc:hc + 2], start=(p == 0), stop=False)
                    last = mm(out, vtok[:, c * P:(c + 1) * P], pd[:, hc:hc + 2], start=False, stop=True)
                last.then_inc(S("pages_used"), 1)
            pe.wait_ge(S("os_ready"), 1)
            for b in range(KB):
                u = U_FS + b
                pe.wait_ge(S(f"raw_in{u % 2}"), 16 * (u // 2 + 1))
                sample_cols(bank(7)[:, b * NS:(b + 1) * NS], u % 2, oS).then_inc(S("fs_used"), 1)
            sample_sums(3)
            pe.wait_ge(S("r2_ready"), 2 * KB)
            pe.wait_ge(S("fg2_ready"), 2 * KB)
            for t in range(TT):
                ln_forward(t, r2T, TT)


def kernel(**inputs):
    import numpy as np
    import concourse.bacc as bacc
    from concourse.bass_utils import run_bass_kernel_spmd as run

    x = {k: np.asarray(a) for k, a in inputs.items()}

    def blocks(w):
        k, n = w.shape
        return w.reshape(k // D, KB, P, n // P, P).transpose(3, 0, 2, 1, 4)

    w_in = blocks(x["cm_w_in"][0])[:, 0]
    kv = x["kv_w"]
    w_f = np.concatenate([kv[:, 2 * D:], np.zeros((D, P - H), kv.dtype)], axis=1)
    fa = blocks(x["fa_w_in"][0])[:, 0]
    kvb = blocks(kv[:, :2 * D])[:, 0]
    w_out = blocks(x["cm_w_out"][0])
    units = np.concatenate([
        w_in[WB:2 * WB],
        np.stack([w_in[2 * WB:], w_in[:WB]], axis=1).reshape(2 * WB, P, KB, P),
        w_out.reshape(2 * KB, P, KB, P),
        blocks(w_f)[:, 0],
        np.stack([kvb[:KB], fa[:KB], kvb[KB:], fa[KB:]], axis=1).reshape(4 * KB, P, KB, P),
        blocks(x["fa_w_out"][0])[:, 0],
    ])
    ada = np.concatenate([blocks(w)[:, 0] for w in x["w_ada"]])

    def feature(v):
        return np.ascontiguousarray(v).reshape(-1, P).T

    c9 = np.concatenate([x["c_sample"], x["c_prompt"]])
    x_all = np.concatenate([x["x_prompt"][0], x["x_sample"][:, 0]])
    kb, fb = x["kv_b"], x["fa_b_in"][0]
    b_f = np.concatenate([kb[2 * D:], np.zeros(P - H, kb.dtype)])
    rep = WB // x["cm_w_s"].shape[1]
    w00 = np.broadcast_to(np.repeat(x["cm_w_s"][0, :, 0, 0], rep)[None], (P, WB))
    b00 = np.broadcast_to(np.repeat(x["cm_b_s"][0, :, 0], rep)[None], (P, WB))
    cols = np.concatenate([
        feature(x["b_ada"]), feature(x["cm_b_in"][0]), feature(x["cm_b_out"][0]),
        feature(kb[:D]), feature(fb[:D]), feature(kb[D:2 * D]), feature(fb[D:]), feature(b_f),
        feature(x["fa_b_out"][0]), feature(x["ln_g"]), feature(x["ln_b"]),
        feature(x["cm_ln_v_g"][0]), feature(x["cm_ln_v_b"][0]), w00, b00], axis=1)
    arrays = {
        "units": units, "w_ada": ada,
        "c_t": c9.reshape(9, KB, P).transpose(2, 1, 0),
        "x_t": x_all.reshape(TA, KB, P).transpose(2, 1, 0),
        "cols_d": cols,
        "ws_t": x["cm_w_s"][0].transpose(2, 0, 1),
        "bs_row": x["cm_b_s"],
        "ln_rows": np.stack([x["ln_g"][1], x["ln_b"][1]]),
        "table": x["page_table"].reshape(1, NS * NP),
        "cache_k": x["cache_k"].reshape(-1, P, D), "cache_v": x["cache_v"].reshape(-1, P, D),
        "cache_f": x["cache_logf"],
    }
    outs = {"y_out": (T, D), "ys_out": (P, KB, NS), "k_out": (KB, P, T), "v_out": (KB, P, T), "f_out": (H, TA),
            "kqv_s_out": (P, 3, KB, 9), "vn_out": (P, WB, NS)}
    nc = bacc.Bacc("TRN2", target_bir_lowering=False, num_devices=1)
    arrays = {k: np.ascontiguousarray(a) for k, a in arrays.items()}
    args = [nc.dram_tensor(k, a.shape, mybir.dt.from_np(a.dtype), kind="ExternalInput").ap() for k, a in arrays.items()]
    args += [nc.dram_tensor(k, s, F32, kind="ExternalOutput").ap() for k, s in outs.items()]
    trunk(nc, *args)
    r = run(nc, [arrays], core_ids=[0]).results[0]

    def rows(a):
        return np.ascontiguousarray(a.transpose(2, 0, 1)).reshape(1, T, H, HD)

    def decode(a):
        return np.ascontiguousarray(a.transpose(2, 1, 0)).reshape(NS, 1, -1)

    s = r["kqv_s_out"]
    return (r["y_out"].reshape(1, T, D), decode(r["ys_out"]), rows(r["k_out"]), rows(r["v_out"]),
            np.ascontiguousarray(r["f_out"][:, :T].T).reshape(1, T, H),
            decode(s[:, 0, :, :NS]).reshape(NS, 1, H, HD), decode(s[:, 2, :, :NS]).reshape(NS, 1, H, HD),
            np.ascontiguousarray(r["f_out"][:, T:].T).reshape(NS, 1, H),
            decode(r["vn_out"]).reshape(1, NS, 1, W))
```

```python
from contextlib import ExitStack

import concourse.bass as bass
from concourse import mybir

F32 = mybir.dt.float32
F32R = mybir.dt.float32r
BF16 = mybir.dt.bfloat16
I32 = mybir.dt.int32
ACT = mybir.ActivationFunctionType
ALU = mybir.AluOpType
AX = mybir.AxisListType

P = 128
D = 1024
KB = D // P
T = 1024
TT = T // P
NS = 8
TA = T + NS
TH = TA // 3
W = 2 * D
WB = W // P
H = 16
HD = 64
NP = 4
PAST = NP * P
HALF = 512
ALPHA = 4.0 ** 0.25
EPS = 1e-5
SCALE = HD ** -0.5
MASKED = -1e30

U_V, U_ZU, U_OUT, U_F, U_B, U_FA = 0, WB, 3 * WB, 4 * WB, 4 * WB + 1, 4 * WB + 1 + 4 * KB
U_FS = U_FA + KB
N_UNITS = U_FS

COLS = {}
_n = 0
for _name, _k in (("b_ada", 48), ("b_in", 48), ("b_out", 8), ("b_kqvz", 32), ("b_f", 1), ("fa_b_out", 8),
                  ("ln_g", 16), ("ln_b", 16), ("v_g", 16), ("v_b", 16), ("w_s00", 16), ("b_s0", 16)):
    COLS[_name] = (_n, _k)
    _n += _k
N_COLS = _n


def wait(eng, sem, value):
    if isinstance(value, int) and value <= 0:
        return
    eng.wait_ge(sem, value)


def settle(eng, sem):
    eng.sem_inc(sem, 1)


def trunk(nc, units, w_ada0, w_ada, c_t, x_t, cols_d, ws_t, bs_row, ln_rows, table, cache_k, cache_v, cache_f,
          y_out, ys_out, k_out, v_out, f_out, kqv_s_out, vn_out):
    ctx = ExitStack()
    with ctx:
        sems = {}

        def S(name):
            if name not in sems:
                sems[name] = ctx.enter_context(nc.semaphore(name))
            return sems[name]

        BASE = 16512
        R1 = BASE
        R2 = R1 + 2 * KB * TA * 4
        RW = R2 + WB * TA * 4
        R3 = RW + 6 * 4096
        RC = R3 + 45216

        def at(name, shape, dt, offset):
            return nc.alloc_sbuf_tensor_at(name, shape, dt, offset=offset)

        const_end = [RC]

        def const(name, shape, dt=F32):
            n = 1
            for s in shape[1:]:
                n *= s
            t = at(name, shape, dt, const_end[0])
            const_end[0] += (n * (2 if dt == BF16 else 4) + 31) // 32 * 32
            assert const_end[0] <= 229368
            return t

        raw = at("raw", [P, 2, KB, P], F32, RW)
        w_hi = at("w_hi", [P, 2, KB, P], F32R, RW + 8192)
        w_lo = at("w_lo", [P, 2, KB, P], F32R, RW + 16384)

        h_hi = at("h_hi", [P, KB, TA], F32R, R1)
        h_lo = at("h_lo", [P, KB, TA], F32R, R1 + KB * TA * 4)
        xT = at("xT", [P, KB, TA], F32, R1 + KB * TA * 4)
        ada_first = at("ada_first", [P, 4, KB, 512], F32, R2)
        m9 = at("m9", [9, 4, 512], F32, R3 + 20480)
        V = at("V", [P, WB, TT, P], F32, R2 + 512)
        yT = at("yT", [P, WB, TA], F32, R2)
        y_hi = at("y_hi", [P, WB, TA], F32R, R2)
        y_lo = at("y_lo", [P, WB, TA], F32R, R1)
        Cst = at("Cst", [P, WB, P], F32, R3)
        wsT = at("wsT", [P, KB, P], F32, R3 + 8192)
        vcur = at("vcur", [P, 2, TT, P], F32, R3 + 12288)
        tmp0 = at("tmp0", [P, TA], F32, R3 + 20480)
        tmp1 = at("tmp1", [P, TA], F32, R3 + 24608)
        tmps = [tmp0, tmp1]
        sgm = at("sgm", [P, TT, P], F32, R3 + 28736)
        bs_b = at("bs_b", [P, KB, P], F32, R3 + 28736)
        ada_ring = at("ada_ring", [P, 2, KB, P], F32, R3 + 32832)
        m9u = at("m9u", [9, 2, P], F32, R3 + 41088)
        cT = at("cT", [P, KB, 9], F32, R3 + 32832)
        thc = at("thc", [P, KB, 9], F32, R3 + 33344)
        hsf = at("hsf", [P, KB, NS], F32, R3 + 33856)
        vstat = at("vstat", [P, TT, 4, 6], F32, R3 + 34368)
        rT = at("rT", [P, KB, T], F32, R3)
        y_tmp = at("y_tmp", [P, 2, TA], F32R, R3 + 32832)
        xb = at("xb", [P, 2, T], F32, R3 + 32832)
        fg = at("fg", [P, TA], F32, R3 + 41088)
        xhat = at("xhat", [P, 2, KB, P], F32, R1)
        x1f = at("x1f", [P, 2, KB, P], F32, R1 + 8192)
        x_hi = at("x_hi", [P, KB, T], F32R, R2)
        x_lo = at("x_lo", [P, KB, T], F32R, R2 + 32768)
        y2T = at("y2T", [P, KB, T], F32, R1)
        kq_hi = at("kq_hi", [P, 2, 2, T], F32R, R1 + 32768)
        kq_lo = at("kq_lo", [P, 2, 2, T], F32R, R1 + 49152)
        Vhl = at("Vhl", [P, TT, 2, 2, HD], F32R, R3)
        vT = at("vT", [P, T], F32, R3 + 8192)
        kf = at("kf", [P, T], F32, R3 + 12288)
        zth = at("zth", [P, HALF], F32, R3 + 16384)
        zb = at("zb", [P, HALF], F32, R3 + 18432)
        prob = at("prob", [P, T], F32, R3 + 20480)
        pt_hi = at("pt_hi", [P, TT, P], F32R, R3 + 24576)
        pt_lo = at("pt_lo", [P, TT, P], F32R, R3 + 28672)
        ckb = at("ckb", [P, 2, T], F32, R3 + 32768)
        otok = at("otok", [P, TT, P], F32, R3 + 40960)
        fp = at("fp", [H, TA], F32, R3)
        fe = at("fe", [H, TA], F32, R3 + 20480)
        f_ones = at("f_ones", [H, T], F32, R3 + 28672)
        fc = at("fc", [H, T], F32, R3 + 12288)
        y2_hi = at("y2_hi", [P, KB, T], F32R, R1 + 32768)
        y2_lo = at("y2_lo", [P, KB, T], F32R, R2 + 32768)
        r2T = at("r2T", [P, KB, T], F32, R1)
        pages = at("pages", [P, 4, NP, D], F32, R2)
        qtok1 = at("qtok1", [NS, D], F32, R2 + 32768)
        xb2 = at("xb2", [P, 2, T], F32, R3)
        g_row = at("g_row", [P, D], F32, R3 + 8192)
        b_row = at("b_row", [P, D], F32, R3 + 16384)
        fg2 = at("fg2", [P, 2, HALF], F32, R3 + 20480)
        PZ = at("PZ", [P, NP, NS, P], F32, R1 + 32768)
        xh2 = at("xh2", [P, 2, D], F32, R1 + 49152)
        yo = at("yo", [P, 2, D], F32, R1 + 57344)
        qbs = [at("qb0", [P, D], F32, R3 + 16384), at("qb1", [P, D], F32, R3 + 8192)]
        qtok = at("qtok", [NS, D], F32, R3 + 24576)
        omask = at("omask", [P, D], F32, R3 + 24576)
        ktok = at("ktok", [NS, D], F32, R3 + 28672)
        vtok = at("vtok", [NS, D], F32, R3 + 32768)
        qk_new = at("qk_new", [NS, D], F32, R3 + 40960)
        scol = at("scol", [P, NP, NS, H], F32, R3 + 12288)
        fpg = at("fpg", [P, NP, NS, H], F32, R3 + 14336)
        fsw = at("fsw", [P, KB, KB, P], F32, RW)
        fs_row = at("fs_row", [NS, D], F32, R3 + 28672)
        cd = at("cd", [P, PAST + 1], F32, R3 + 40960)
        Ld = at("Ld", [P, PAST + 1], F32, R3 + 43040)
        assert 43040 + 2052 <= 45216

        cols = const("cols", [P, N_COLS])
        ident = const("ident", [P, P])
        identb = const("identb", [P, P], BF16)
        ones = const("ones", [P, P])
        maskb = const("maskb", [P, P], BF16)
        mT = const("mT", [P, 48, 9])
        scT = const("scT", [P, KB, 9])
        one_p = const("one_p", [P, KB])
        xS = const("xS", [P, KB, NS])
        vS = const("vS", [P, WB, NS])
        vnS = const("vnS", [P, WB, NS])
        sq = const("sq", [P, WB, NS])
        sgS = const("sgS", [P, WB, NS])
        rS = const("rS", [P, KB, NS])
        x1S = const("x1S", [P, KB, 9])
        hS = const("hS", [P, KB, 9])
        kqvzS = const("kqvzS", [P, 4, KB, 9])
        red = const("red", [P, NS])
        mean = const("mean", [P, NS])
        rsd = const("rsd", [P, NS])
        mv = const("mv", [P, TT, 2])
        vr = const("vr", [P, TT])
        vnm = const("vnm", [P, TT])
        hbz = const("hbz", [P, WB])
        g1 = const("g1", [P, KB])
        gb = const("gb", [P, KB])
        gS = const("gS", [P, KB, NS])
        lst = const("lst", [P, 2, 6])
        lmv = const("lmv", [P, 2, 2])
        lr = const("lr", [P, 2])
        lnm = const("lnm", [P, 2])
        nmin = const("nmin", [P, 2])
        rsum = const("rsum", [P, 2])
        rcp = const("rcp", [P, 2])
        otmp = const("otmp", [P, HD])
        hbz2 = const("hbz2", [P, 1])
        fS = const("fS", [H, NS])
        mask8 = const("mask8", [NS, NS, H])
        maskp = const("maskp", [P, NS])
        ex = at("ex", [NS, 2, NS, H], F32, R3 + 38912)
        sn = at("sn", [NS, 2, H], F32, R3 + 40448)
        pd = at("pd", [NS, P], F32, R3 + 39936)
        pdx = at("pdx", [P, NS], F32, R3 + 40576)
        hm = at("hm", [P, H], F32, R3 + 40864)
        dn = const("dn", [P, 4])
        oS = at("oS", [P, KB, NS], F32, R3 + 40608)
        ptab = const("ptab", [1, NS * NP], I32)

        def col(name, i=None):
            a, n = COLS[name]
            return cols[:, a:a + n] if i is None else cols[:, a + i:a + i + 1]

        def col_at(name, i):
            a, _ = COLS[name]
            return cols[:, bass.ds(a + i, 1)] if not isinstance(i, int) else col(name, i)

        def wide(ap, n):
            return ap.rearrange("p (a o) -> p a o", o=1).broadcast_to([ap.shape[0], ap.shape[1], n])

        def over(ap, n):
            return ap.rearrange("p (o b) -> p o b", o=1).broadcast_to([ap.shape[0], n, ap.shape[1]])

        ps = [ctx.enter_context(nc.psum_tensor(f"bank{i}{i + 1}", [P, 2, 512], F32)) for i in (0, 2, 4, 6)]

        def bank(b):
            return ps[b // 2][:, b % 2, :]

        SUMS = {1: 3, 2: 7, 3: 4}

        def pair(n):
            return ps[n][:, :, :].rearrange("p a b -> p (a b)")

        def third(s, t):
            return bank(3 * s + t)[:, 0:TH]

        def thirds(eng_op, s, sb, *rest):
            for t in range(3):
                last = eng_op(t, third(s, t), sb[:, t * TH:(t + 1) * TH], *rest)
            return last

        scr_x = nc.dram_tensor("scr_x", [KB, P, T], F32, kind="Internal").ap()
        scr_c = nc.dram_tensor("scr_c", [H, T], F32, kind="Internal").ap()
        scr_q = nc.dram_tensor("scr_q", [NS, D], F32, kind="Internal").ap()

        block = ctx.enter_context(nc.Block())

        @block.sync
        def _(sp):
            sp.dma_start(cT[:, :, :], c_t).then_inc(S("c_in"), 16)
            sp.dma_start(cols[:, :], cols_d).then_inc(S("cols_in"), 16)
            for g in range(4):
                for h in range(2):
                    sp.dma_start(ada_first[:, g, 4 * h:4 * h + 4, :], w_ada0[:, g, 4 * h:4 * h + 4, :])\
                      .then_inc(S(f"ada_in{g}"), 16)
            sp.dma_start(xT[:, :, :], x_t).then_inc(S("x_in"), 16)
            sp.dma_start(wsT[:, :, :], ws_t).then_inc(S("ws_in"), 16)
            sp.dma_start(bs_b[:, :, :], bs_row.broadcast_to([P, KB, P])).then_inc(S("ws_in"), 16)
            sp.dma_start(ptab[:, :], table).then_inc(S("table_in"), 16)

            def load(u, slot, i=None):
                wait(sp, S("lo_ready"), u - 1)
                sp.dma_start(raw[:, slot, :, :], units[u, :, :, :]).then_inc(S(f"raw_in{slot}"), 16)

            load(0, 0)
            load(1, 1)
            with sp.Fori(0, WB // 2 - 1) as i:
                for s in range(2):
                    load(2 * i + 2 + s, s)
            for j in range(1):
                for s in range(2):
                    load(U_ZU + s, s)
                for s in range(2):
                    if s == 0:
                        sp.wait_ge(S("v_norm"), 1)
                    sp.dma_start(ada_ring[:, s, :, :], w_ada[s, :, :, :]).then_inc(S(f"ada_ring_in{s}"), 16)
            with sp.Fori(1, WB) as j:
                for s in range(2):
                    load(U_ZU + 2 * j + s, s)
                for s in range(2):
                    sp.wait_ge(S("ada_used"), 2 * j - 1 + s)
                    sp.dma_start(ada_ring[:, s, :, :], w_ada[2 * j + s, :, :, :])\
                      .then_inc(S(f"ada_ring_in{s}"), 16)
            for b in range(KB):
                for s in range(2):
                    if b != 1 or s != 0:
                        load(U_OUT + 2 * b + s, s)
                if b == 0:
                    load(U_OUT + 2, 0)
                    sp.wait_ge(S("y_lo_ready"), WB)
                if b >= 2:
                    sp.wait_ge(S("r_ready"), b - 1)
                sp.dma_start(xb[:, b % 2, :], x_t[:, b, 0:T]).then_inc(S(f"xb_in{b % 2}"), 16)
            load(U_F, 0)

            def load_b(m, s):
                wait(sp, S("mm"), 3 * m - 5)
                if isinstance(m, int) and m == 1:
                    sp.wait_ge(S("f_mm"), 1)
                settle(sp, S("settled"))
                load(U_B + m, s)

            for m in range(4):
                load_b(m, (m + 1) % 2)
            with sp.Fori(1, KB) as j:
                for q in range(4):
                    load_b(4 * j + q, (q + 1) % 2)
            for b in range(KB):
                if b == 0:
                    sp.wait_ge(S("mm"), 12 * KB - 5)
                if b == 1:
                    sp.wait_ge(S("mm"), 12 * KB - 2)
                load(U_FA + b, (U_FA + b) % 2)
                if b == 0:
                    sp.wait_ge(S("v_hl"), KB)
                    sp.wait_ge(S("pv_done"), 16 * KB)
                if b >= 2:
                    sp.wait_ge(S("r2_ready"), 2 * b - 2)
                sp.wait_ge(S("scr_x_out0"), 16 * TT // 2)
                sp.wait_ge(S("scr_x_out1"), 16 * TT // 2)
                sp.dma_start(xb2[:, b % 2, :], scr_x[b, :, :]).then_inc(S(f"xb2_in{b % 2}"), 16)
            sp.wait_ge(S("pages_used"), NS)
            sp.dma_start(g_row[:, :], ln_rows[0:1, :].broadcast_to([P, D])).then_inc(S("rows_in"), 16)
            sp.dma_start(b_row[:, :], ln_rows[1:2, :].broadcast_to([P, D])).then_inc(S("rows_in"), 16)
            sp.wait_ge(S("r2_ready"), 2 * KB)
            sp.wait_ge(S("lo_ready"), U_FS)
            sp.wait_ge(S("fa_mm"), 2 * KB)
            for b in range(KB):
                sp.dma_start(fsw[:, b, :, :], units[U_FA + b, :, :, :]).then_inc(S("fsw_in"), 16)
            for t in range(TT):
                sp.wait_ge(S("yo_ready"), t + 1)
                sp.dma_start(y_out[t * P:(t + 1) * P, :], yo[:, t % 2, :]).then_inc(S(f"y_out{t % 2}"), 16)
            sp.wait_ge(S("y_out0"), 16 * TT // 2)
            sp.wait_ge(S("y_out1"), 16 * TT // 2)
            sp.wait_ge(S("ys_ready"), 1)
            sp.dma_start(ys_out, rS[:, :, :]).then_inc(S("ys_out"), 16)
            sp.wait_ge(S("ys_out"), 16)

        @block.gpsimd
        def _(pool):
            g = nc.gpsimd
            g.memset(ident[:, :], 1.0).then_inc(S("pc"), 1)
            g.memset(ones[:, :], 1.0).then_inc(S("pc"), 1)
            g.memset(maskb[:, :], MASKED).then_inc(S("pc"), 1)
            g.memset(identb[:, :], 1.0).then_inc(S("pc"), 1)
            g.memset(mask8[:, :, :], 1.0).then_inc(S("pc"), 1)
            g.memset(maskp[:, :], 1.0).then_inc(S("pc"), 1)
            pool.wait_ge(S("pc"), 6)
            for m in (ident, identb):
                g.affine_select(out=m[:, :], in_=m[:, :], compare_op=ALU.is_equal, fill=0.0, base=0,
                                pattern=[[-1, P]], channel_multiplier=1).then_inc(S("consts"), 1)
            g.affine_select(out=maskb[:, :], in_=maskb[:, :], compare_op=ALU.is_gt, fill=0.0, base=0,
                            pattern=[[1, P]], channel_multiplier=-1).then_inc(S("consts"), 1)
            g.affine_select(out=mask8[:, :, :], in_=mask8[:, :, :], compare_op=ALU.is_equal, fill=0.0, base=0,
                            pattern=[[1, NS], [0, H]], channel_multiplier=-1).then_inc(S("consts"), 1)
            g.affine_select(out=maskp[:, :], in_=maskp[:, :], compare_op=ALU.is_ge, fill=0.0, base=0,
                            pattern=[[-H, NS]], channel_multiplier=1).then_inc(S("pc"), 1)
            pool.wait_ge(S("pc"), 7)
            g.affine_select(out=maskp[:, :], in_=maskp[:, :], compare_op=ALU.is_ge, fill=0.0, base=H - 1,
                            pattern=[[H, NS]], channel_multiplier=-1).then_inc(S("consts"), 1)
            pool.wait_ge(S("ws_in"), 32)
            g.affine_select(out=wsT[:, :, :], in_=wsT[:, :, :], compare_op=ALU.is_ge, fill=0.0, base=0,
                            pattern=[[0, KB], [1, P]], channel_multiplier=-1).then_inc(S("ws_ready"), 1)
            def norm_v(j, s):
                wait(pool, S("spatial_done"), j - 1)
                pool.wait_ge(S("v_norm"), 1)
                g.tensor_tensor(vcur[:, s, :, :], V[:, j, :, :], wide(vr[:, :], P), ALU.mult).then_inc(S("vcur_mul"), 1)
                pool.wait_ge(S("vcur_mul"), j + 1)
                g.tensor_tensor(vcur[:, s, :, :], vcur[:, s, :, :], wide(vnm[:, :], P), ALU.add)\
                    .then_inc(S("vcur_ready"), 1)

            pool.wait_ge(S("v_norm"), 1)
            norm_v(0, 0)
            norm_v(1, 1)
            with pool.Fori(1, WB // 2) as i:
                for s in range(2):
                    norm_v(2 * i + s, s)
            pool.wait_ge(S("vn_s"), 1)
            pool.dma_start(vn_out, vnS[:, :, :]).then_inc(S("vn_out"), 16)
            for t in range(TT):
                pool.wait_ge(S("x1f_ready"), t + 1)
                pool.wait_ge(S("x1f_upper"), t + 1)
                pool.dma_start(scr_x[:, :, t * P:(t + 1) * P].rearrange("k p t -> p k t"), x1f[:, t % 2, :, :])\
                    .then_inc(S(f"scr_x_out{t % 2}"), 16)
                pool.wait_ge(S("x1_hi"), t + 1)
                g.tensor_tensor(x_lo[:, :, t * P:(t + 1) * P], x1f[:, t % 2, :, :],
                                x_hi[:, :, t * P:(t + 1) * P].bitcast(F32), ALU.subtract).then_inc(S("x1_ready"), 1)
            pool.wait_ge(S("f_ready"), 1)
            pool.dma_start(f_out, fp[:, :]).then_inc(S("f_out"), 16)
            pool.wait_ge(S("c_ready"), 1)
            pool.dma_start(scr_c, fc[:, :]).then_inc(S("scr_c"), 16)
            pool.wait_ge(S("scr_c"), 16)

            def load_c(j, h):
                pool.dma_start(ckb[:, h, :], scr_c[bass.ds(2 * j + h, 1), :].broadcast_to([P, T])
                               if not isinstance(j, int) else scr_c[2 * j + h:2 * j + h + 1, :].broadcast_to([P, T]))\
                    .then_inc(S(f"ckb_in{h}"), 16)

            def store_kv(j, par):
                pool.wait_ge(S("evac"), 12 * j + 3)
                wait(pool, S("k_out"), 16 * j)
                g.tensor_tensor(kf[:, :], kq_hi[:, par, 0, :].bitcast(F32), kq_lo[:, par, 0, :].bitcast(F32), ALU.add)\
                    .then_inc(S("kf_ready"), 1)
                pool.wait_ge(S("kf_ready"), j + 1)
                pool.dma_start(k_out[j, :, :], kf[:, :]).then_inc(S("k_out"), 16)
                pool.wait_ge(S("evac"), 12 * j + 9)
                settle(pool, S("settled"))
                pool.dma_start(v_out[j, :, :], vT[:, :]).then_inc(S("v_out"), 16)

            pool.wait_ge(S("f_out"), 16)
            load_c(0, 0)
            load_c(0, 1)
            store_kv(0, 0)

            def phase(j, par):
                store_kv(j + 1, 1 - par)
                for h in range(2):
                    pool.wait_ge(S("nl_ready"), 16 * j + 15 + h)
                    load_c(j + 1, h)

            phase(0, 0)
            with pool.Fori(0, KB // 2 - 1) as i2:
                phase(2 * i2 + 1, 1)
                phase(2 * i2 + 2, 0)
            pool.wait_ge(S("evac"), 12 * KB)
            pool.dma_start(kqv_s_out, kqvzS[:, 0:3, :, :]).then_inc(S("kqv_s_out"), 16)

            pool.wait_ge(S("table_in"), 16)
            pool.wait_ge(S("mm"), 12 * KB)

            def load_set(cache, b, s):
                for p in range(NP):
                    page = pool.value_load(ptab[0:1, bass.ds(b * NP + p, 1)], min_val=0, max_val=cache_k.shape[0] - 1)
                    pool.dma_start(pages[:, s, p, :], cache[bass.ds(page, 1), :, :].rearrange("a p c -> p (a c)"))\
                        .then_inc(S(f"pages_in{s}"), 16)

            def load_f(b):
                for p in range(NP):
                    page = pool.value_load(ptab[0:1, bass.ds(b * NP + p, 1)], min_val=0, max_val=cache_f.shape[0] - 1)
                    pool.dma_start(fpg[:, p, b, :], cache_f[bass.ds(page, 1), :, :].rearrange("a p h -> p (a h)"))\
                        .then_inc(S("fpg_in"), 16)

            def load_q(b, s):
                wait(pool, S("qk_prod"), NP * (b - 1))
                settle(pool, S("settled"))
                row = scr_q[b:b + 1, :] if isinstance(b, int) else scr_q[bass.ds(b, 1), :]
                pool.dma_start(qbs[s][:, :], row.broadcast_to([P, D])).then_inc(S(f"qb_in{s}"), 16)

            load_set(cache_k, 0, 0)
            pool.wait_ge(S("tok_ready"), 1)
            pool.dma_start(scr_q, qtok1[:, :]).then_inc(S("scr_q"), 16)
            load_set(cache_k, 1, 1)
            pool.wait_ge(S("scr_q"), 16)
            pool.wait_ge(S("zs_done"), 2 * KB)
            pool.wait_ge(S("v_out"), 16 * KB)
            pool.wait_ge(S("k_out"), 16 * KB)
            load_q(0, 0)
            load_q(1, 1)
            load_f(0)
            load_f(1)
            with pool.Fori(1, NS // 2) as i:
                for s in range(2):
                    load_q(2 * i + s, s)
                    pool.wait_ge(S("pages_used"), 2 * i + s - 1)
                    load_set(cache_k, 2 * i + s, s)
                    load_f(2 * i + s)
            for b in range(NS):
                if b < 2:
                    pool.wait_ge(S("pages_used"), NS - 1 + b)
                elif b == 2:
                    pool.wait_ge(S("fa_mm"), 2 * KB)
                elif b >= 4:
                    pool.wait_ge(S("pages_used"), NS + b - 3)
                load_set(cache_v, b, b % 4)
            for name, n in (("vn_out", 16), ("k_out", 16 * KB), ("v_out", 16 * KB), ("kqv_s_out", 16)):
                pool.wait_ge(S(name), n)

        @block.scalar
        def _(act):
            A = nc.scalar.activation

            def hi(u, slot, n, free="hl_used", value=None):
                act.wait_ge(S(f"raw_in{slot}"), 16 * n)
                wait(act, S(free), u - 1 if value is None else value)
                A(w_hi[:, slot, :, :], raw[:, slot, :, :], ACT.Copy).then_inc(S("hi_ready"), 1)

            def hi_scaled(u, slot, n, free, value, part=None):
                if part != 1:
                    act.wait_ge(S(f"raw_in{slot}"), 16 * n)
                    wait(act, S(free), value)
                for k in range(KB) if part is None else range(part * KB // 2, (part + 1) * KB // 2):
                    last = A(w_hi[:, slot, k, :], raw[:, slot, k, :], ACT.Copy, scale=one_p[:, k:k + 1])
                if part != 0:
                    last.then_inc(S("hi_ready"), 1)

            act.wait_ge(S("c_in"), 16)
            A(thc[:, :, :], cT[:, :, :], ACT.Tanh, scale=0.5).then_inc(S("thc"), 1)
            act.wait_ge(S("hs_ready"), 1)
            A(h_hi[:, :, T:TA], hsf[:, :, :], ACT.Copy).then_inc(S("hs_hi"), 1)
            hi(0, 0, 1)
            for k in range(KB):
                act.wait_ge(S("hf_ready"), k + 1)
                A(h_hi[:, k, 0:T], tmps[k % 2][:, 0:T], ACT.Copy).then_inc(S("h_hi_ready"), 1)

            def gelu_v(j, s):
                act.wait_ge(S("hl_used"), U_V + j + 1)
                wait(act, S("v_tr"), j - 1)
                wait(act, S("v_s"), j - 1)
                for t in range(3):
                    last = A(tmps[s][:, t * TH:(t + 1) * TH], third(s, t), ACT.Gelu_apprx_tanh,
                             bias=col_at("b_in", WB + j))
                last.then_inc(S("v_act"), 1)

            act.wait_ge(S("h_ready"), KB)
            for j in range(2):
                hi(j + 1, (j + 1) % 2, (j + 1) // 2 + 1)
                gelu_v(j, j % 2)
            with act.Fori(1, WB // 2) as i:
                for s in range(2):
                    hi(2 * i + s + 1, 1 - s, i + 1 + s)
                    gelu_v(2 * i + s, s)
            act.wait_ge(S("v_var"), 1)
            A(vr[:, :], vr[:, :], ACT.Sqrt).then_inc(S("v_sqrt"), 1)

            def sqrt_s(n):
                act.wait_ge(S("s_var"), n)
                A(rsd[:, :], rsd[:, :], ACT.Sqrt).then_inc(S("s_sqrt"), 1)

            sqrt_s(1)

            def act_zu(j):
                hi(U_ZU + 2 * j + 1, 1, WB // 2 + j + 1)
                act.wait_ge(S("hl_used"), U_ZU + 2 * j + 1)
                wait(act, S("y_ready"), j)
                for t in range(3):
                    last = A(tmp0[:, t * TH:(t + 1) * TH], third(0, t), ACT.Tanh, bias=hbz[:, bass.ds(j, 1)], scale=0.5)
                last.then_inc(S("z_th"), 1)
                hi(U_ZU + 2 * j + 2, 0, WB // 2 + j + 2)
                act.wait_ge(S("ada_used"), 2 * j + 2)
                for t in range(3):
                    last = A(tmp1[:, t * TH:(t + 1) * TH], third(1, t), ACT.Gelu_apprx_tanh, bias=col_at("b_in", j))
                last.then_inc(S("u_act"), 1)

            act.wait_ge(S("v_tr"), WB)
            act.wait_ge(S("v_s"), WB)
            act_zu(0)
            with act.Fori(1, WB) as j:
                act_zu(j)

            def odd_y_hi(k):
                act.wait_ge(S("y_lo_ready"), k + 1)
                A(y_hi[:, k, :], yT[:, k, :], ACT.Copy).then_inc(S("y_split_odd"), 1)

            for k in range(WB):
                if k == 0:
                    act.wait_ge(S("ada_used"), 2 * WB)
                act.wait_ge(S("y_ready"), k + 1)
                wait(act, S("y_lo_ready"), k - 1)
                A(y_tmp[:, k % 2, :], yT[:, k, :], ACT.Copy).then_inc(S("y_tmp_ready"), 1)
                if k % 2 == 0 and k > 0:
                    odd_y_hi(k - 1)
                if k in (2, 13):
                    u = U_OUT + (1 if k == 2 else 2)
                    hi(u, u % 2, u // 2 + 1)
            odd_y_hi(WB - 1)
            for b in range(KB):
                for s in range(2):
                    u = U_OUT + 2 * b + s + 1
                    if u > U_OUT + 2:
                        hi(u, u % 2, u // 2 + 1)
                if b == 0:
                    act.wait_ge(S("gate_ready"), 1)
                act.wait_ge(S("hl_used"), U_OUT + 2 * b + 2)
                wait(act, S("r_ready"), b)
                for t in range(3):
                    last = A(fg[:, t * TH:(t + 1) * TH], third(b % 2, t), ACT.Identity,
                             bias=gb[:, b:b + 1], scale=g1[:, b:b + 1])
                last.then_inc(S("fg_ready"), 1)

            def layer_norm_act(t, n0, dst, free):
                act.wait_ge(S("ln_var"), n0 + t + 1)
                A(lr[:, t % 2:t % 2 + 1], lr[:, t % 2:t % 2 + 1], ACT.Sqrt).then_inc(S("ln_sqrt"), 1)
                act.wait_ge(S("ln_stat"), n0 + t + 1)
                wait(act, S(free), t - 1)
                A(dst, pair(t % 2), ACT.Identity, bias=lnm[:, t % 2:t % 2 + 1], scale=lr[:, t % 2:t % 2 + 1])\
                    .then_inc(S("ln_hat"), 1)

            def x1_back_act(t):
                act.wait_ge(S("ln1_back"), t + 1)
                if t >= 2:
                    act.wait_ge(S(f"scr_x_out{t % 2}"), 16 * (t // 2))
                    act.wait_ge(S("x1_hi"), t - 1)
                    act.wait_ge(S("x1_ready"), t - 1)
                for k in range(KB // 2, KB):
                    last = A(x1f[:, t % 2, k, :], pair(2 + t % 2)[:, k * P:(k + 1) * P], ACT.Identity,
                             bias=col("ln_b", k), scale=col("ln_g", k))
                last.then_inc(S("x1f_upper"), 1)

            def x1_hi(t):
                act.wait_ge(S("x1f_ready"), t + 1)
                act.wait_ge(S("x1f_upper"), t + 1)
                if t == 0:
                    act.wait_ge(S("hl_used"), U_OUT + 2 * KB)
                A(x_hi[:, :, t * P:(t + 1) * P], x1f[:, t % 2, :, :], ACT.Copy).then_inc(S("x1_hi"), 1)

            def split_hi(j, q, *part):
                u = U_B + 4 * j + q
                n = 2 * j + (U_B + q) // 2 + 1
                free = ("hl_used", u - 1) if isinstance(j, int) and 4 * j + q < 2 else ("mm", 12 * j + 3 * q - 3)
                (hi_scaled if q in (1, 3) else hi)(u, (U_B + q) % 2, n, *free, *part)

            split_hi(0, 0)
            for t in range(TT):
                layer_norm_act(t, 0, xhat[:, t % 2, :, :].rearrange("p a b -> p (a b)"), "ln1_back")
                if t == 1:
                    sqrt_s(2)
                if t >= 1:
                    x1_back_act(t - 1)
                    x1_hi(t - 1)
            x1_back_act(TT - 1)
            x1_hi(TT - 1)

            act.wait_ge(S("f_abs"), 1)
            A(fe[:, :], fe[:, :], ACT.Exp, scale=-1.0).then_inc(S("f_exp"), 1)
            act.wait_ge(S("f_exp"), 1)
            A(fe[:, :], fe[:, :], ACT.Ln, bias=1.0).then_inc(S("f_ln"), 1)


            def evac_hi(j, q, half, par):
                act.wait_ge(S("mm"), 12 * j + 3 * q + half + 2)
                src = bank((q + half + 1) % 2)
                cs = slice(half * HALF, half * HALF + HALF)
                if q == 0:
                    wait(act, S("s_done"), 16 * j - 16)
                    wait(act, S("kf_ready"), j - 1)
                    settle(act, S("settled"))
                    A(kq_hi[:, par, 0, cs], src, ACT.Identity, bias=col_at("b_kqvz", j)).then_inc(S("ev_hi"), 1)
                elif q == 1:
                    act.wait_ge(S("evac"), 12 * j + 4)
                    settle(act, S("settled"))
                    A(kq_hi[:, par, 1, cs], src, ACT.Identity, bias=kqvzS[:, 1, j, 8:9]).then_inc(S("ev_hi"), 1)
                elif q == 3:
                    if half == 0:
                        act.wait_ge(S("hbz_ready"), j + 1)
                    wait(act, S("zs_done"), 2 * j + half)
                    A(zth[:, :], src, ACT.Tanh, bias=hbz2[:, 0:1], scale=0.5).then_inc(S("ev_hi"), 1)

            def v_hi(j):
                act.wait_ge(S("vt_done"), j + 1)
                wait(act, S("pv_done"), 16 * j)
                A(Vhl[:, :, :, 0, :], pair(2).rearrange("p (t h d) -> p t h d", t=TT, h=2), ACT.Copy)\
                    .then_inc(S("v_hi"), 1)

            def pt_high(j, i):
                nk = i // 2 + 1
                act.wait_ge(S("t_done"), 16 * j + i + 1)
                wait(act, S("pv_done"), 16 * j + i)
                A(pt_hi[:, 0:nk, :], pair(2)[:, 0:nk * P], ACT.Copy).then_inc(S("pt_hi"), 1)

            def exp(j, i):
                nk = i // 2 + 1
                act.wait_ge(S("nl_ready"), 16 * j + i + 1)
                wait(act, S("rcp_ready"), 16 * j + max(i - 1, 0))
                A(prob[:, 0:nk * P], prob[:, 0:nk * P], ACT.Exp, bias=nmin[:, i % 2:i % 2 + 1], scale=-1.0,
                  accum_out=rsum[:, i % 2:i % 2 + 1]).then_inc(S("p_ready"), 1)

            def o_part(j, i):
                act.wait_ge(S("pv_done"), 16 * j + i + 1)
                act.wait_ge(S("rcp_ready"), 16 * j + i + 1)
                wait(act, S("o_evac"), 16 * j + i)
                A(otmp[:, :], bank(6 + i % 2)[:, HD:2 * HD], ACT.Copy, scale=rcp[:, i % 2:i % 2 + 1])\
                    .then_inc(S("otmp_ready"), 1)

            for q in range(4):
                split_hi((q + 1) // 4, (q + 1) % 4)
                if q != 2:
                    for half in range(2):
                        evac_hi(0, q, half, 0)
            act.wait_ge(S("f_out"), 16)
            v_hi(0)

            HALVES = {2: (0, 0), 5: (0, 1), 7: (1, 0), 10: (1, 1), 13: (2, 0), 15: (2, 1)}

            def y2_high(k):
                act.wait_ge(S("y2_ready"), k + 1)
                A(y2_hi[:, k, :], y2T[:, k, :], ACT.Copy).then_inc(S("y2_hi"), 1)

            def phase(j, par, more):
                for i in range(16):
                    if i >= 1:
                        pt_high(j, i - 1)
                    exp(j, i)
                    if more and i in HALVES and HALVES[i][0] != 2:
                        evac_hi(j + 1, *HALVES[i], 1 - par)
                    if more and i in (1, 2, 6, 11, 12):
                        split_hi(j + 1, *{1: (1, 0), 2: (1, 1), 6: (2,), 11: (3, 0), 12: (3, 1)}[i])
                    if i >= 1:
                        o_part(j, i - 1)
                    if not more and i in (11, 13):
                        if i == 11:
                            act.wait_ge(S("s_done"), 16 * (KB - 1))
                            act.wait_ge(S("kf_ready"), KB - 1)
                        y2_high((i - 11) // 2)
                pt_high(j, 15)
                o_part(j, 15)
                if more:
                    split_hi(j + 2, 0)
                    evac_hi(j + 1, 3, 0, 1 - par)
                    v_hi(j + 1)
                    evac_hi(j + 1, 3, 1, 1 - par)

            phase(0, 0, True)
            with act.Fori(0, KB // 2 - 1) as i2:
                phase(2 * i2 + 1, 1, True)
                phase(2 * i2 + 2, 0, True)
            phase(KB - 1, 1, False)

            act.wait_ge(S("y2_ready"), KB)
            act.wait_ge(S("s_done"), 16 * KB)
            act.wait_ge(S("kf_ready"), KB)
            for k in range(2, KB):
                y2_high(k)
            for b in range(KB):
                if b + 1 < KB:
                    u = U_FA + b + 1
                    hi(u, u % 2, u // 2 + 1, *(("fa_mm", 2 * b) if b else ("mm", 12 * KB)))
                for half in range(2):
                    n = 2 * b + half
                    act.wait_ge(S("fa_mm"), n + 1)
                    wait(act, S("r2_ready"), n - 1)
                    A(fg2[:, half, :], bank(half), ACT.Identity, bias=gb[:, b:b + 1], scale=g1[:, b:b + 1])\
                        .then_inc(S("fg2_ready"), 1)
            for p in range(NP):
                A(PZ[:, p, :, :], over(ones[:, :], NS), ACT.Copy, scale=0.0).then_inc(S("pz_zero"), 1)
            act.wait_ge(S("d_max"), 1)
            A(Ld[:, :], Ld[:, :], ACT.Exp, bias=dn[:, 0:1], accum_out=dn[:, 1:2]).then_inc(S("d_exp"), 1)
            A(sq[:, 0:KB, :], kqvzS[:, 3, :, 0:NS], ACT.Tanh, scale=0.5).then_inc(S("zs_th"), 1)

            for t in range(TT):
                layer_norm_act(t, TT, xh2[:, t % 2, :], "yo_ready")
            sqrt_s(3)

        @block.vector
        def _(dve):
            v = nc.vector
            chain = [0]

            def link(ins):
                chain[0] += 1
                ins.then_inc(S("dve_chain"), 1)
                dve.wait_ge(S("dve_chain"), chain[0])

            def lo(u, slot):
                dve.wait_ge(S("hi_ready"), u + 1)
                v.tensor_tensor(w_lo[:, slot, :, :], raw[:, slot, :, :], w_hi[:, slot, :, :].bitcast(F32), ALU.subtract)\
                    .then_inc(S("lo_ready"), 1)

            def lo_scaled(u, slot, part=None):
                dve.wait_ge(S("hi_ready"), u + 1)
                for k in range(KB) if part is None else range(part * KB // 2, (part + 1) * KB // 2):
                    last = v.scalar_tensor_tensor(w_lo[:, slot, k, :], raw[:, slot, k, :], one_p[:, k:k + 1],
                                                  w_hi[:, slot, k, :].bitcast(F32), ALU.mult, ALU.subtract)
                if part != 0:
                    last.then_inc(S("lo_ready"), 1)

            dve.wait_ge(S("c_in"), 16)
            dve.wait_ge(S("thc"), 1)
            link(v.scalar_tensor_tensor(scT[:, :, :], thc[:, :, :], 1.0, cT[:, :, :], ALU.add, ALU.mult))
            v.tensor_scalar(scT[:, :, :], scT[:, :, :], 0.5, None, ALU.mult).then_inc(S("sc_ready"), 1)
            dve.wait_ge(S("cols_in"), 16)
            v.tensor_scalar(hbz[:, :], cols[:, COLS["b_in"][0] + 2 * WB:COLS["b_in"][0] + 3 * WB], 0.5, None, ALU.mult)
            for g in range(4):
                dve.wait_ge(S("ada0_mm"), g + 1)
                v.tensor_copy(m9[:, g, :], bank(g)[0:9, :]).then_inc(S("m9_ready"), 1)
            dve.wait_ge(S("ada0_mm"), 5)
            link(v.tensor_tensor(mT[:, 0:16, :], bank(4)[:, 0:16 * 9].rearrange("p (a n) -> p a n", n=9),
                                 wide(cols[:, 0:16], 9), ALU.add))
            link(v.tensor_scalar(one_p[:, :], mT[:, 8:16, 8], 1.0, None, ALU.add))
            dve.wait_ge(S("x_in"), 16)
            v.tensor_copy(xS[:, :, :], xT[:, :, T:TA])
            link(v.tensor_scalar(hsf[:, :, :], mT[:, 8:16, 0:NS], 1.0, None, ALU.add))
            link(v.tensor_tensor(hsf[:, :, :], hsf[:, :, :], xT[:, :, T:TA], ALU.mult))
            v.tensor_tensor(hsf[:, :, :], hsf[:, :, :], mT[:, 0:8, 0:NS], ALU.add).then_inc(S("hs_ready"), 1)
            dve.wait_ge(S("hs_hi"), 1)
            v.tensor_tensor(h_lo[:, :, T:TA], hsf[:, :, :], h_hi[:, :, T:TA].bitcast(F32), ALU.subtract)
            lo(0, 0)

            def h_low(k):
                dve.wait_ge(S("h_hi_ready"), k + 1)
                v.tensor_tensor(h_lo[:, k, 0:T], tmps[k % 2][:, 0:T], h_hi[:, k, 0:T].bitcast(F32), ALU.subtract)\
                    .then_inc(S("h_ready"), 1)

            for k in range(KB):
                wait(dve, S("h_ready"), k - 1)
                v.tensor_scalar(tmps[k % 2][:, 0:T], xT[:, k, 0:T], one_p[:, k:k + 1], mT[:, k, 8:9], ALU.mult, ALU.add)\
                    .then_inc(S("hf_ready"), 1)
                if k >= 1:
                    h_low(k - 1)
            h_low(KB - 1)
            lo(1, 1)
            dve.wait_ge(S("rs_mm"), 1)
            dve.wait_ge(S("ws_in"), 32)
            for j in range(WB):
                g = j // 2
                last = v.scalar_tensor_tensor(Cst[:, j, :], pair(3)[:, g * P:(g + 1) * P], col("v_b", j),
                                              bs_b[:, g, :], ALU.mult, ALU.add)
            last.then_inc(S("cst_ready"), 1)

            def store_v(j, s):
                dve.wait_ge(S("v_act"), j + 1)
                v.tensor_copy(vS[:, j, :], tmps[s][:, T:TA]).then_inc(S("v_s"), 1)
                dve.wait_ge(S("v_tr"), j + 1)
                v.tensor_copy(V[:, j, :, :], pair(3).rearrange("p (t c) -> p t c", c=P)).then_inc(S("v_stored"), 1)

            def stats(jq):
                dve.wait_ge(S("v_stored"), 4 * jq + 4)
                for t in range(TT):
                    last = v.bn_stats(vstat[:, t, jq, :], V[:, 4 * jq:4 * jq + 4, t, :])
                return last

            for j in range(WB):
                if j + 2 <= U_ZU:
                    lo(j + 2, j % 2)
                store_v(j, j % 2)
                if j % 4 == 3:
                    last = stats(j // 4)
            link(last)
            for t in range(TT):
                last = v.bn_aggr(mv[:, t, :], vstat[:, t, :, :].rearrange("p a b -> p (a b)"))
            link(last)
            v.tensor_scalar(vr[:, :], mv[:, :, 1], EPS, None, ALU.add).then_inc(S("v_var"), 1)
            dve.wait_ge(S("v_sqrt"), 1)
            link(v.reciprocal(vr[:, :], vr[:, :]))
            v.scalar_tensor_tensor(vnm[:, :], mv[:, :, 0], -1.0, vr[:, :], ALU.mult, ALU.mult).then_inc(S("v_norm"), 1)

            def sample_norm(n, x, nb, gname, g0, bname, out):
                link(v.tensor_reduce(red[:, :], x.rearrange("p b n -> p n b"), AX.X, ALU.add))
                v.tensor_scalar(red[:, :], red[:, :], 1.0 / (nb * P), None, ALU.mult).then_inc(S("s_sum"), 1)
                dve.wait_ge(S("s_mm"), 2 * n - 1)
                link(v.tensor_copy(mean[:, :], bank(SUMS[n])[:, 0:NS]))
                link(v.tensor_tensor(out, x, over(mean[:, :], nb), ALU.subtract))
                link(v.tensor_tensor(sq[:, 0:nb, :], out, out, ALU.mult))
                link(v.tensor_reduce(red[:, :], sq[:, 0:nb, :].rearrange("p b n -> p n b"), AX.X, ALU.add))
                v.tensor_scalar(red[:, :], red[:, :], 1.0 / (nb * P), None, ALU.mult).then_inc(S("s_sum"), 1)
                dve.wait_ge(S("s_mm"), 2 * n)
                v.tensor_scalar(rsd[:, :], bank(SUMS[n])[:, 0:NS], EPS, None, ALU.add).then_inc(S("s_var"), 1)
                dve.wait_ge(S("s_sqrt"), n)
                link(v.reciprocal(rsd[:, :], rsd[:, :]))
                link(v.tensor_tensor(out, out, over(rsd[:, :], nb), ALU.mult))
                a, b = COLS[gname][0] + g0, COLS[bname][0] + g0
                link(v.tensor_tensor(out, out, wide(cols[:, a:a + nb], NS), ALU.mult))
                return v.tensor_tensor(out, out, wide(cols[:, b:b + nb], NS), ALU.add)

            link(sample_norm(1, vS[:, :, :], WB, "v_g", 0, "v_b", vnS[:, :, :]))
            link(v.tensor_tensor(sgS[:, :, :], vnS[:, :, :], wide(col("w_s00"), NS), ALU.mult))
            v.tensor_tensor(sgS[:, :, :], sgS[:, :, :], wide(col("b_s0"), NS), ALU.add).then_inc(S("vn_s"), 1)

            def modulation(src, n):
                return v.tensor_tensor(mT[:, bass.ds(n, 2), :], src.rearrange("p (a n) -> p a n", n=9),
                                       cols[:, bass.ds(n, 2)].rearrange("p (a o) -> p a o", o=1).broadcast_to([P, 2, 9]),
                                       ALU.add)

            def dve_zu(j):
                lo(U_ZU + 2 * j + 1, 1)
                dve.wait_ge(S("z_th"), j + 1)
                if not isinstance(j, int):
                    modulation(bank(2)[:, 360:378], 14 + 2 * j)
                v.tensor_scalar(tmp0[:, :], tmp0[:, :], 1.0, None, ALU.add).then_inc(S("z_th1"), 1)
                dve.wait_ge(S("z_th1"), j + 1)
                for t in range(3):
                    last = v.scalar_tensor_tensor(tmp0[:, t * TH:(t + 1) * TH], third(0, t), col_at("b_in", 2 * WB + j),
                                                  tmp0[:, t * TH:(t + 1) * TH], ALU.add, ALU.mult)
                last.then_inc(S("z_silu"), 1)
                dve.wait_ge(S("spatial_done"), j + 1)
                wait(dve, S("y_ready"), j)
                v.scalar_tensor_tensor(sgm[:, :, :], pair(3).rearrange("p (t c) -> p t c", c=P), col_at("v_g", j),
                                       Cst[:, bass.ds(j, 1), :].broadcast_to([P, TT, P]), ALU.mult, ALU.add)\
                    .then_inc(S("sgm_ready"), 1)
                lo(U_ZU + 2 * j + 2, 0)
                dve.wait_ge(S("u_act"), j + 1)
                dve.wait_ge(S("z_silu"), j + 1)
                v.tensor_tensor(tmp0[:, :], tmp0[:, :], tmp1[:, :], ALU.mult).then_inc(S("uz_ready"), 1)
                v.tensor_copy(m9u[:, :, :], ps[2][0:9, :, TH:TH + P]).then_inc(S("ada_ev"), 1)
                dve.wait_ge(S("uz_ready"), j + 1)
                dve.wait_ge(S("sgm_ready"), j + 1)
                v.scalar_tensor_tensor(yT[:, j, T:TA], tmp0[:, T:TA], 0.5, sgS[:, j, :], ALU.mult, ALU.mult)
                v.scalar_tensor_tensor(yT[:, j, 0:T], tmp0[:, 0:T], 0.5, sgm[:, :, :].rearrange("p t c -> p (t c)"),
                                       ALU.mult, ALU.mult).then_inc(S("y_ready"), 1)

            dve.wait_ge(S("cst_ready"), 1)
            dve.wait_ge(S("vn_s"), 1)
            dve_zu(0)
            with dve.Fori(1, WB) as j:
                dve_zu(j)

            for k in range(WB):
                dve.wait_ge(S("y_tmp_ready"), k + 1)
                if k == 0:
                    dve.wait_ge(S("hl_used"), U_OUT)
                v.tensor_tensor(y_lo[:, k, :], yT[:, k, :], y_tmp[:, k % 2, :].bitcast(F32), ALU.subtract)\
                    .then_inc(S("y_lo_ready"), 1)
                if k % 2 == 0:
                    dve.wait_ge(S("y_lo_ready"), k + 1)
                    v.tensor_copy(y_hi[:, k, :], yT[:, k, :]).then_inc(S("y_split"), 1)
                if k in (2, 13):
                    u = U_OUT + (1 if k == 2 else 2)
                    lo(u, u % 2)

            def gates(layer, bname):
                a = 24 * layer + 16
                link(v.tensor_scalar(g1[:, :], mT[:, a:a + 8, 8], 1.0, None, ALU.add))
                v.tensor_scalar(gS[:, :, :], mT[:, a:a + 8, 0:NS], 1.0, None, ALU.add)
                link(v.tensor_tensor(gb[:, :], g1[:, :], col(bname), ALU.mult))

            dve.wait_ge(S("ada0_mm"), 6)
            link(modulation(bank(6)[:, 0:18], 14 + 2 * WB))
            gates(0, "b_out")
            v.tensor_scalar(one_p[:, :], mT[:, 32:40, 8], 1.0, None, ALU.add).then_inc(S("gate_ready"), 1)
            for b in range(KB):
                for s in range(2):
                    u = U_OUT + 2 * b + s + 1
                    if u > U_OUT + 2:
                        lo(u, u % 2)
                dve.wait_ge(S("fg_ready"), b + 1)
                dve.wait_ge(S(f"xb_in{b % 2}"), 16 * (b // 2 + 1))
                v.tensor_scalar(rS[:, b, :], bank(3 * (b % 2) + 2)[:, TH - NS:TH], col("b_out", b), None, ALU.add)
                v.scalar_tensor_tensor(rT[:, b, :], xb[:, b % 2, :], ALPHA, fg[:, 0:T], ALU.mult, ALU.add)\
                    .then_inc(S("r_ready"), 1)

            dve.wait_ge(S("r_ready"), KB)

            def residual_s(x):
                link(v.tensor_tensor(rS[:, :, :], rS[:, :, :], gS[:, :, :], ALU.mult))
                link(v.scalar_tensor_tensor(rS[:, :, :], x, ALPHA, rS[:, :, :], ALU.mult, ALU.add))

            def layer_norm_stats(t, n0):
                dve.wait_ge(S("ln_tr"), n0 + t + 1)
                for h in range(2):
                    last = v.bn_stats(lst[:, h, :], ps[t % 2][:, h, :])
                link(last)
                wait(dve, S("ln_hat"), n0 + t - 1)
                link(v.bn_aggr(lmv[:, t % 2, :], lst[:, :, :].rearrange("p a b -> p (a b)")))
                v.tensor_scalar(lr[:, t % 2:t % 2 + 1], lmv[:, t % 2, 1:2], EPS, None, ALU.add)\
                    .then_inc(S("ln_var"), 1)
                dve.wait_ge(S("ln_sqrt"), n0 + t + 1)
                link(v.reciprocal(lr[:, t % 2:t % 2 + 1], lr[:, t % 2:t % 2 + 1]))
                v.scalar_tensor_tensor(lnm[:, t % 2:t % 2 + 1], lmv[:, t % 2, 0:1], -1.0, lr[:, t % 2:t % 2 + 1],
                                       ALU.mult, ALU.mult).then_inc(S("ln_stat"), 1)

            def x1_back(t):
                dve.wait_ge(S("ln1_back"), t + 1)
                if t >= 2:
                    dve.wait_ge(S(f"scr_x_out{t % 2}"), 16 * (t // 2))
                    dve.wait_ge(S("x1_hi"), t - 1)
                    dve.wait_ge(S("x1_ready"), t - 1)
                for k in range(KB // 2):
                    last = v.tensor_scalar(x1f[:, t % 2, k, :], pair(2 + t % 2)[:, k * P:(k + 1) * P],
                                           col("ln_g", k), col("ln_b", k), ALU.mult, ALU.add)
                last.then_inc(S("x1f_ready"), 1)

            def split_lo(j, q, *part):
                (lo_scaled if q in (1, 3) else lo)(U_B + 4 * j + q, (U_B + q) % 2, *part)

            def decode_in():
                residual_s(xS[:, :, :])
                link(sample_norm(2, rS[:, :, :], KB, "ln_g", 0, "ln_b", x1S[:, :, 0:NS]))
                v.tensor_copy(x1S[:, :, 8], mT[:, 24:32, 8])
                v.tensor_copy(hS[:, :, 8], mT[:, 24:32, 8])
                link(v.tensor_scalar(hS[:, :, 0:NS], mT[:, 32:40, 0:NS], 1.0, None, ALU.add))
                link(v.tensor_tensor(hS[:, :, 0:NS], hS[:, :, 0:NS], x1S[:, :, 0:NS], ALU.mult))
                v.tensor_tensor(hS[:, :, 0:NS], hS[:, :, 0:NS], mT[:, 24:32, 0:NS], ALU.add).then_inc(S("s_in"), 1)

            for t in range(TT):
                layer_norm_stats(t, 0)
                if t == 2:
                    split_lo(0, 0)
                if t >= 1:
                    x1_back(t - 1)
                if t == 1:
                    decode_in()
            x1_back(TT - 1)

            dve.wait_ge(S("f_mm"), 1)
            for half in range(2):
                v.tensor_scalar(fp[:, half * HALF:(half + 1) * HALF], bank(half)[0:H, :], cols[0:H, COLS["b_f"][0]:COLS["b_f"][0] + 1],
                                None, ALU.add)
            v.tensor_scalar(fp[:, T:TA], bank(2)[0:H, 0:NS], cols[0:H, COLS["b_f"][0]:COLS["b_f"][0] + 1], None, ALU.add)\
                .then_inc(S("f_evac"), 1)
            dve.wait_ge(S("f_evac"), 1)
            v.tensor_scalar(fe[:, :], fp[:, :], -1.0, None, ALU.mult).then_inc(S("f_neg"), 1)
            dve.wait_ge(S("f_neg"), 1)
            v.tensor_tensor(fe[:, :], fe[:, :], fp[:, :], ALU.max).then_inc(S("f_abs"), 1)
            v.memset(f_ones[:, :], 1.0)
            dve.wait_ge(S("f_ln"), 1)
            v.scalar_tensor_tensor(fp[:, :], fp[:, :], 0.0, fe[:, :], ALU.min, ALU.subtract).then_inc(S("f_ready"), 1)
            dve.wait_ge(S("f_ready"), 1)
            v.tensor_copy(fS[:, :], fp[:, T:TA])
            link(v.tensor_tensor_scan(fc[:, :], f_ones[:, :], fp[:, 0:T], 0.0, ALU.mult, ALU.add))
            v.tensor_scalar(fc[:, :], fc[:, :], -1.0 / SCALE, None, ALU.mult).then_inc(S("c_ready"), 1)


            def evac_s(j, q):
                dve.wait_ge(S("mm"), 12 * j + 3 * q + 1)
                v.tensor_scalar(kqvzS[:, q, j, :], bank(q % 2)[:, 0:9], col_at("b_kqvz", q * KB + j), None, ALU.add)\
                    .then_inc(S("evac"), 1)
                if q == 3:
                    dve.wait_ge(S("evac"), 12 * j + 3 * q + 1)
                    wait(dve, S("ev_hi"), 6 * j)
                    v.tensor_scalar(hbz2[:, :], kqvzS[:, 3, j, 8:9], 0.5, None, ALU.mult).then_inc(S("hbz_ready"), 1)

            EV = {0: 0, 1: 2, 3: 4}

            def evac_lo(j, q, half, par):
                src = bank((q + half + 1) % 2)
                cs = slice(half * HALF, half * HALF + HALF)
                if q == 2:
                    dve.wait_ge(S("mm"), 12 * j + 3 * q + half + 2)
                    wait(dve, S("v_out"), 16 * j)
                    wait(dve, S("vt_done"), j)
                    v.tensor_scalar(vT[:, cs], src, col_at("b_kqvz", 2 * KB + j), None, ALU.add).then_inc(S("evac"), 1)
                    return
                dve.wait_ge(S("ev_hi"), 6 * j + EV[q] + half + 1)
                if q == 0:
                    v.scalar_tensor_tensor(kq_lo[:, par, 0, cs], src, col_at("b_kqvz", j),
                                           kq_hi[:, par, 0, cs].bitcast(F32), ALU.add, ALU.subtract).then_inc(S("evac"), 1)
                elif q == 1:
                    v.scalar_tensor_tensor(kq_lo[:, par, 1, cs], src, kqvzS[:, 1, j, 8:9],
                                           kq_hi[:, par, 1, cs].bitcast(F32), ALU.add, ALU.subtract).then_inc(S("evac"), 1)
                else:
                    wait(dve, S("zs_done"), 2 * j + half)
                    if isinstance(j, int) and j == 0:
                        for t in range(2):
                            dve.wait_ge(S(f"scr_x_out{t}"), 16 * TT // 2)
                    v.tensor_scalar(zb[:, :], src, kqvzS[:, 3, j, 8:9], 0.5, ALU.add, ALU.mult).then_inc(S("evac"), 1)
                    dve.wait_ge(S("evac"), 12 * j + 3 * q + half + 2)
                    v.scalar_tensor_tensor(y2T[:, j, cs], zth[:, :], 1.0, zb[:, :], ALU.add, ALU.mult)\
                        .then_inc(S("zs_done"), 1)

            def v_lo(j):
                dve.wait_ge(S("v_hi"), j + 1)
                v.tensor_tensor(Vhl[:, :, :, 1, :], pair(2).rearrange("p (t h d) -> p t h d", t=TT, h=2),
                                Vhl[:, :, :, 0, :].bitcast(F32), ALU.subtract).then_inc(S("v_hl"), 1)

            def y2_low(k):
                if k == 0:
                    dve.wait_ge(S("scr_q"), 16)
                dve.wait_ge(S("y2_hi"), k + 1)
                v.tensor_tensor(y2_lo[:, k, :], y2T[:, k, :], y2_hi[:, k, :].bitcast(F32), ALU.subtract)\
                    .then_inc(S("y2_split"), 1)

            def tok(n, dst, src):
                dve.wait_ge(S("tok_mm"), n)
                v.tensor_copy(dst[:, :], pair(src)[0:NS, :]).then_inc(S("tok_ready"), 1)

            def score(n):
                b, p = divmod(n, NP)
                if n == 0:
                    dve.wait_ge(S("k_out"), 16 * KB)
                if p == 0:
                    dve.wait_ge(S(f"pages_in{b % 2}"), 16 * NP * (b // 2 + 1))
                    dve.wait_ge(S(f"qb_in{b % 2}"), 16 * (b // 2 + 1))
                v.tensor_tensor(pages[:, b % 2, p, :], pages[:, b % 2, p, :], qbs[b % 2][:, :], ALU.mult)\
                    .then_inc(S("qk_prod"), 1)
                dve.wait_ge(S("qk_prod"), n + 1)
                last = v.tensor_reduce(scol[:, p, b, :], pages[:, b % 2, p, :].rearrange("p (h d) -> p h d", d=HD), AX.X, ALU.add)
                if p == NP - 1:
                    last.then_inc(S("pages_used"), 1)

            EARLY = 11

            def logits(j, i):
                nk = i // 2 + 1
                dve.wait_ge(S("s_done"), 16 * j + i + 1)
                if i < 2:
                    dve.wait_ge(S(f"ckb_in{i}"), 16 * j + 16)
                wait(dve, S("t_done"), 16 * j + i)
                settle(dve, S("settled"))
                v.tensor_tensor_reduce(out=prob[:, 0:nk * P], in0=pair(1)[:, 0:nk * P], in1=ckb[:, i % 2, 0:nk * P],
                                       scale=-SCALE, scalar=3e38, op0=ALU.add, op1=ALU.min,
                                       accum_out=nmin[:, i % 2:i % 2 + 1]).then_inc(S("nl_ready"), 1)

            def pt_low(j, i):
                nk = i // 2 + 1
                dve.wait_ge(S("pt_hi"), 16 * j + i + 1)
                v.tensor_tensor(pt_lo[:, 0:nk, :], pair(2)[:, 0:nk * P].rearrange("p (t c) -> p t c", c=P),
                                pt_hi[:, 0:nk, :].bitcast(F32), ALU.subtract).then_inc(S("pt_ready"), 1)
                dve.wait_ge(S("p_ready"), 16 * j + i + 1)
                wait(dve, S("otmp_ready"), 16 * j + max(i - 1, 0))
                v.reciprocal(rcp[:, i % 2:i % 2 + 1], rsum[:, i % 2:i % 2 + 1]).then_inc(S("rcp_ready"), 1)

            def o_full(j, i):
                dve.wait_ge(S("otmp_ready"), 16 * j + i + 1)
                if i == 0:
                    wait(dve, S("ot_done"), j)
                v.scalar_tensor_tensor(otok[:, i // 2, (i % 2) * HD:(i % 2 + 1) * HD], bank(6 + i % 2)[:, 0:HD],
                                       rcp[:, i % 2:i % 2 + 1], otmp[:, :], ALU.mult, ALU.add).then_inc(S("o_evac"), 1)

            def gate_o(j):
                dve.wait_ge(S("ot_done"), j + 1)
                dve.wait_ge(S("zs_done"), 2 * j + 2)
                v.tensor_tensor(y2T[:, j, :], pair(1), y2T[:, j, :], ALU.mult).then_inc(S("y2_ready"), 1)

            for q in range(4):
                split_lo((q + 1) // 4, (q + 1) % 4)
                evac_s(0, q)
                for half in range(2):
                    evac_lo(0, q, half, 0)
            v_lo(0)

            HALVES = {2: (0, 0), 5: (0, 1), 7: (1, 0), 10: (1, 1), 13: (2, 0), 15: (2, 1)}

            def phase(j, par, more):
                for i in range(16):
                    if i >= 1:
                        pt_low(j, i - 1)
                    logits(j, i)
                    if more and i == 0:
                        evac_s(j + 1, 0)
                    if more and i in HALVES:
                        evac_lo(j + 1, *HALVES[i], 1 - par)
                    if more and i in (5, 10):
                        evac_s(j + 1, i // 5)
                    if more and i in (3, 4, 7, 13, 14):
                        split_lo(j + 1, *{3: (1, 0), 4: (1, 1), 7: (2,), 13: (3, 0), 14: (3, 1)}[i])
                    if not more and i >= 16 - EARLY:
                        score(i - 16 + EARLY)
                    if i >= 1:
                        o_full(j, i - 1)
                    if not more and i == 0:
                        tok(1, qtok1, 0)
                    if not more and i in (11, 13):
                        y2_low((i - 11) // 2)
                pt_low(j, 15)
                o_full(j, 15)
                if more:
                    evac_s(j + 1, 3)
                    split_lo(j + 2, 0)
                    evac_lo(j + 1, 3, 0, 1 - par)
                    v_lo(j + 1)
                gate_o(j)
                if more:
                    evac_lo(j + 1, 3, 1, 1 - par)

            phase(0, 0, True)
            with dve.Fori(0, KB // 2 - 1) as i2:
                phase(2 * i2 + 1, 1, True)
                phase(2 * i2 + 2, 0, True)
            phase(KB - 1, 1, False)

            gates(1, "fa_b_out")
            for k in range(2, KB):
                y2_low(k)
            def new_key():
                dve.wait_ge(S("tok_ready"), 4)
                link(v.tensor_tensor(qk_new[:, :], qtok[:, :], ktok[:, :], ALU.mult))
                link(v.tensor_reduce(sn[:, 0, :], qk_new[:, :].rearrange("p (h d) -> p h d", d=HD), AX.X, ALU.add))
                dve.wait_ge(S("tok_mm"), 5)
                link(v.tensor_copy(sn[:, 1, :], bank(6)[0:NS, 0:H]))
                for c in range(2):
                    last = v.tensor_tensor(ex[:, c, :, :], over(sn[:, c, :], NS), mask8[:, :, :], ALU.mult)
                last.then_inc(S("sn_ready"), 1)

            def decay():
                dve.wait_ge(S("d_tr"), 1)
                v.tensor_copy(Ld[:, 0:PAST], bank(4))
                dve.wait_ge(S("d_new"), 1)
                link(v.tensor_copy(dn[:, 2:4], bank(6)[:, 0:2]))
                link(v.tensor_copy(Ld[:, PAST:PAST + 1], dn[:, 3:4]))
                link(v.tensor_tensor_scan(cd[:, :], ones[:, 0:1].broadcast_to([P, PAST + 1]), Ld[:, :], 0.0, ALU.mult, ALU.add))

            taken = EARLY
            for b in range(KB):
                if b + 1 < KB:
                    lo(U_FA + b + 1, (U_FA + b + 1) % 2)
                for half in range(2):
                    n = 2 * b + half
                    dve.wait_ge(S("fg2_ready"), n + 1)
                    if half == 0:
                        dve.wait_ge(S(f"xb2_in{b % 2}"), 16 * (b // 2 + 1))
                    v.scalar_tensor_tensor(r2T[:, b, half * HALF:(half + 1) * HALF], xb2[:, b % 2, half * HALF:(half + 1) * HALF],
                                           ALPHA, fg2[:, half, :], ALU.mult, ALU.add).then_inc(S("r2_ready"), 1)
                    for m in range(2 if n in (0, 1, 2, 4, 6, 8) else 1 if n < 15 else 0):
                        score(taken)
                        taken += 1
                    if n == 10:
                        tok(2, qtok, 2)
                        tok(3, ktok, 3)
                    if n == 12:
                        tok(4, vtok, 2)
                        new_key()
                    if n == 14:
                        decay()

            assert taken == NS * NP
            dve.wait_ge(S("d_tr"), 2)
            v.scalar_tensor_tensor(Ld[:, PAST:PAST + 1], dn[:, 2:3], SCALE, cd[:, PAST:PAST + 1], ALU.mult, ALU.subtract)
            link(v.scalar_tensor_tensor(Ld[:, 0:PAST], bank(5), SCALE, cd[:, 0:PAST], ALU.mult, ALU.subtract))
            v.tensor_reduce(dn[:, 0:1], Ld[:, :], AX.X, ALU.max, negate=True).then_inc(S("d_max"), 1)
            dve.wait_ge(S("d_exp"), 1)
            link(v.reciprocal(dn[:, 1:2], dn[:, 1:2]))
            link(v.tensor_scalar(Ld[:, :], Ld[:, :], dn[:, 1:2], None, ALU.mult))
            v.tensor_scalar(pdx[:, :], maskp[:, :], Ld[:, PAST:PAST + 1], None, ALU.mult).then_inc(S("d_p"), 1)
            dve.wait_ge(S("d_tr"), 3)
            dve.wait_ge(S("pz_zero"), NP)
            for b in range(NS):
                v.tensor_copy(PZ[:, :, b, b * H:(b + 1) * H], bank(4).rearrange("p (a b) -> p a b", b=P)[:, :, b * H:(b + 1) * H])
            v.tensor_copy(pd[:, :], bank(5)[0:NS, 0:P]).then_inc(S("d_pt"), 1)
            link(v.tensor_reduce(hm[:, :], ident[:, :].rearrange("p (b h) -> p h b", h=H), AX.X, ALU.add))
            dve.wait_ge(S("zs_th"), 1)
            link(v.scalar_tensor_tensor(sq[:, 0:KB, :], sq[:, 0:KB, :], 1.0, kqvzS[:, 3, :, 0:NS], ALU.add, ALU.mult))

            dve.wait_ge(S("rows_in"), 32)

            def finish(t):
                dve.wait_ge(S("ln_hat"), TT + t + 1)
                v.tensor_tensor(xh2[:, t % 2, :], xh2[:, t % 2, :], g_row[:, :], ALU.mult).then_inc(S("ln2_mul"), 1)
                dve.wait_ge(S("ln2_mul"), t + 1)
                if t >= 2:
                    dve.wait_ge(S(f"y_out{t % 2}"), 16 * (t // 2))
                v.tensor_tensor(yo[:, t % 2, :], xh2[:, t % 2, :], b_row[:, :], ALU.add).then_inc(S("yo_ready"), 1)

            for t in range(TT):
                layer_norm_stats(t, TT)
                if t >= 1:
                    finish(t - 1)
            finish(TT - 1)

            dve.wait_ge(S("pages_used"), 2 * NS)
            dve.wait_ge(S("d_pv"), 1)
            v.tensor_tensor(omask[:, :].rearrange("p (h d) -> p h d", d=HD), pair(3).rearrange("p (h d) -> p h d", d=HD),
                            wide(hm[:, :], HD), ALU.mult).then_inc(S("om_ready"), 1)
            dve.wait_ge(S("d_o"), 1)
            v.scalar_tensor_tensor(oS[:, :, :], bank(4)[:, 0:KB * NS].rearrange("p (a b) -> p a b", b=NS), 0.5,
                                   sq[:, 0:KB, :], ALU.mult, ALU.mult).then_inc(S("os_ready"), 1)
            for h in range(2):
                dve.wait_ge(S("fs_used"), h + 1)
                v.tensor_copy(fs_row[:, h * 512:(h + 1) * 512], bank(6 + h)[0:NS, :]).then_inc(S("fs_row"), 1)
            dve.wait_ge(S("fs_used"), 3)
            link(v.tensor_tensor(rS[:, :, :], bank(5)[:, 0:KB * NS].rearrange("p (a b) -> p a b", b=NS),
                                 wide(col("fa_b_out"), NS), ALU.add))
            residual_s(x1S[:, :, 0:NS])
            sample_norm(3, rS[:, :, :], KB, "ln_g", KB, "ln_b", rS[:, :, :]).then_inc(S("ys_ready"), 1)

        @block.tensor
        def _(pe):
            mm = nc.tensor.matmul

            def three(out, lhs_hi, lhs_lo, rhs_hi, rhs_lo, first, last):
                mm(out, lhs_lo, rhs_hi, start=first, stop=False)
                mm(out, lhs_hi, rhs_lo, start=False, stop=False)
                return mm(out, lhs_hi, rhs_hi, start=False, stop=last)

            pe.wait_ge(S("sc_ready"), 1)
            for g in range(4):
                pe.wait_ge(S(f"ada_in{g}"), 32)
                for k in range(KB):
                    last = mm(bank(g)[0:9, :], scT[:, k, :], ada_first[:, g, k, :], start=(k == 0), stop=(k == KB - 1))
                last.then_inc(S("ada0_mm"), 1)
            pe.wait_ge(S("consts"), 5)
            for g in range(4):
                pe.wait_ge(S("m9_ready"), g + 1)
                for a in range(4 * g, 4 * g + 4):
                    last = mm(bank(4)[:, a * 9:a * 9 + 9], m9[:, g, (a % 4) * P:(a % 4 + 1) * P], ident[0:9, 0:9],
                              start=True, stop=True)
            last.then_inc(S("ada0_mm"), 1)
            pe.wait_ge(S("ws_ready"), 1)
            for h in range(2):
                last = mm(ps[3][:, h, :], ones[:, :], wsT[:, 4 * h:4 * h + 4, :], start=True, stop=True)
            last.then_inc(S("rs_mm"), 1)

            def block_a(u, slot, s, k0=0, rhs=(h_hi, h_lo), nk=KB, waits=None):
                pe.wait_ge(S("lo_ready"), u + 1)
                for k in range(KB):
                    if waits == "y_split":
                        pe.wait_ge(S("y_split"), (k0 + k) // 2 + 1)
                        wait(pe, S("y_split_odd"), (k0 + k + 1) // 2)
                    elif waits:
                        pe.wait_ge(S(waits), k0 + k + 1)
                    for t in range(3):
                        last = three(third(s, t), w_hi[:, slot, k, :], w_lo[:, slot, k, :],
                                     rhs[0][:, k0 + k, t * TH:(t + 1) * TH], rhs[1][:, k0 + k, t * TH:(t + 1) * TH],
                                     k0 + k == 0, k0 + k == nk - 1)
                return last

            def transpose_v(j, s):
                pe.wait_ge(S("v_act"), j + 1)
                wait(pe, S("v_stored"), j)
                for t in range(TT):
                    last = nc.tensor.transpose(pair(3)[:, t * P:(t + 1) * P], tmps[s][:, t * P:(t + 1) * P], ident[:, :])
                last.then_inc(S("v_tr"), 1)

            def block_v(j, s, waits=None):
                wait(pe, S("v_act"), j - 1)
                last = block_a(j, s, s, waits=waits)
                last.then_inc(S("hl_used"), 1)

            block_v(0, 0, "h_ready")
            block_v(1, 1)
            pe.wait_ge(S("cst_ready"), 1)
            transpose_v(0, 0)
            with pe.Fori(1, WB // 2) as i:
                for s in range(2):
                    block_v(2 * i + s, s)
                    transpose_v(2 * i + s - 1, 1 - s)
            transpose_v(WB - 1, 1)

            def sample_sums(n):
                for i in range(2):
                    pe.wait_ge(S("s_sum"), 2 * n - 1 + i)
                    mm(bank(SUMS[n])[:, 0:NS], ones[:, :], red[:, :], start=True, stop=True).then_inc(S("s_mm"), 1)

            def turn_ada(out, n):
                pe.wait_ge(S("ada_ev"), n)
                for a in range(2):
                    last = mm(out[:, 9 * a:9 * a + 9], m9u[:, a, :], ident[0:9, 0:9], start=True, stop=True)
                return last

            def block_zu(j, s):
                wait(pe, S("z_silu"), j) if not isinstance(j, int) or j else pe.wait_ge(S("v_act"), WB)
                last = block_a(U_ZU + 2 * j, 0, 0)
                if not isinstance(j, int) or j:
                    last = turn_ada(bank(2)[:, 360:378], j)
                last.then_inc(S("hl_used"), 1)
                if isinstance(j, int) and j == 0:
                    sample_sums(1)
                pe.wait_ge(S("vcur_ready"), j + 1)
                wait(pe, S("sgm_ready"), j) if not isinstance(j, int) or j else pe.wait_ge(S("v_stored"), WB)
                g = j // 2 if isinstance(j, int) else None
                for t in range(TT):
                    rhs = wsT[:, g, :] if g is not None else wsT[:, bass.ds(block_zu.g, 1), :].rearrange("p a c -> p (a c)")
                    last = mm(pair(3)[:, t * P:(t + 1) * P], vcur[:, s, t, :], rhs, start=True, stop=True)
                last.then_inc(S("spatial_done"), 1)
                if not isinstance(j, int) or j:
                    wait(pe, S("u_act"), j)
                    wait(pe, S("ada_ev"), j)
                else:
                    pe.wait_ge(S("s_var"), 1)
                block_a(U_ZU + 2 * j + 1, 1, 1).then_inc(S("hl_used"), 1)
                for a in range(2):
                    pe.wait_ge(S(f"ada_ring_in{a}"), 16 * (j + 1))
                    for k in range(KB):
                        last = mm(bank(4 + a)[0:9, TH:TH + P], scT[:, k, :], ada_ring[:, a, k, :],
                                  start=(k == 0), stop=(k == KB - 1))
                    last.then_inc(S("ada_used"), 1)

            block_zu(0, 0)
            block_zu(1, 1)
            with pe.Fori(1, WB // 2) as i:
                block_zu.g = i
                for s in range(2):
                    block_zu(2 * i + s, s)

            pe.wait_ge(S("sgm_ready"), WB)
            turn_ada(bank(6), WB).then_inc(S("ada0_mm"), 1)

            def block_out(b, s, waits=None):
                if b < 2:
                    pe.wait_ge(S("z_silu" if b == 0 else "ada_ev"), WB)
                    if b == 1:
                        pe.wait_ge(S("u_act"), WB)
                else:
                    pe.wait_ge(S("r_ready"), b - 1)
                block_a(U_OUT + 2 * b, 0, s, 0, (y_hi, y_lo), WB, waits).then_inc(S("hl_used"), 1)
                last = block_a(U_OUT + 2 * b + 1, 1, s, KB, (y_hi, y_lo), WB, waits)
                last.then_inc(S("hl_used"), 1)

            for b in range(KB):
                block_out(b, b % 2, "y_split" if b == 0 else None)

            pe.wait_ge(S("r_ready"), KB)
            def ln_forward(t, src, n0):
                wait(pe, S("ln_hat"), n0 + t - 1)
                for k in range(KB):
                    last = nc.tensor.transpose(pair(t % 2)[:, k * P:(k + 1) * P], src[:, k, t * P:(t + 1) * P], ident[:, :])
                last.then_inc(S("ln_tr"), 1)

            def ln_backward(t):
                pe.wait_ge(S("ln_hat"), t + 1)
                wait(pe, S("x1f_ready"), t - 1)
                if t == 1:
                    pe.wait_ge(S("s_var"), 2)
                for k in range(KB):
                    last = nc.tensor.transpose(pair(2 + t % 2)[:, k * P:(k + 1) * P], xhat[:, t % 2, k, :], ident[:, :])
                last.then_inc(S("ln1_back"), 1)

            ln_forward(0, rT, 0)
            ln_forward(1, rT, 0)
            for t in range(TT):
                ln_backward(t)
                if t == 0:
                    sample_sums(2)
                if t + 2 < TT:
                    ln_forward(t + 2, rT, 0)

            def sample_cols(out, slot, src):
                for k in range(KB):
                    last = mm(out, raw[:, slot, k, :], src[:, k, :], start=(k == 0), stop=(k == KB - 1))
                return last

            def token_step(out, slot, half, k):
                cs = slice(half * HALF, half * HALF + HALF)
                return three(out, w_hi[:, slot, k, :], w_lo[:, slot, k, :], x_hi[:, k, cs], x_lo[:, k, cs],
                             k == 0, k == KB - 1)

            pe.wait_ge(S("lo_ready"), U_F + 1)
            for half in range(2):
                pe.wait_ge(S("x1_ready"), TT // 2 * (half + 1))
                for k in range(KB):
                    last = token_step(bank(half), 0, half, k)
            last.then_inc(S("hl_used"), 1)
            pe.wait_ge(S("s_in"), 1)
            sample_cols(bank(2)[:, 0:9], 0, x1S).then_inc(S("f_mm"), 1)

            def step(j, q, n):
                slot = (U_B + q) % 2
                half, k = divmod(n, KB)
                if n == 0:
                    wait(pe, S("evac"), 12 * j + 3 * q - 1)
                    pe.wait_ge(S("lo_ready"), U_B + 4 * j + q + 1)
                    last = sample_cols(bank(q % 2)[:, 0:9], slot, hS if q in (1, 3) else x1S)
                    last.then_inc(S("mm"), 1)
                if k == 0:
                    wait(pe, S("evac"), 12 * j + 3 * q + half)
                last = token_step(bank((q + half + 1) % 2), slot, half, k)
                if k == KB - 1:
                    last.then_inc(S("mm"), 1)

            def transpose_vt(j):
                pe.wait_ge(S("evac"), 12 * j + 9)
                wait(pe, S("pt_ready"), 16 * j)
                for t in range(TT):
                    last = nc.tensor.transpose(pair(2)[:, t * P:(t + 1) * P], vT[:, t * P:(t + 1) * P], ident[:, :])
                last.then_inc(S("vt_done"), 1)

            def scores(j, i, par):
                qt, h = divmod(i, 2)
                nk = qt + 1
                rows = slice(h * HD, (h + 1) * HD)
                qs = slice(qt * P, (qt + 1) * P)
                if i == 0:
                    pe.wait_ge(S("evac"), 12 * j + 6)
                    wait(pe, S("y2_ready"), j)
                wait(pe, S("nl_ready"), 16 * j + i)
                for c in range((nk + 3) // 4):
                    n = min(4, nk - 4 * c) * P
                    ks = slice(c * 512, c * 512 + n)
                    out = ps[1][:, c, 0:n]
                    end = c == (nk - 1) // 4
                    mm(out, kq_lo[rows, par, 1, qs], kq_hi[rows, par, 0, ks], start=True, stop=False)
                    mm(out, kq_hi[rows, par, 1, qs], kq_lo[rows, par, 0, ks], start=False, stop=False)
                    mm(out, kq_hi[rows, par, 1, qs], kq_hi[rows, par, 0, ks], start=False, stop=not end)
                mm(pair(1)[:, qt * P:(qt + 1) * P], identb[:, :], maskb[:, :], start=False, stop=True)\
                    .then_inc(S("s_done"), 1)

            def turn(q, n):
                for c in range(KB):
                    last = mm(pair(n)[0:NS, c * P:(c + 1) * P], kqvzS[:, q, c, 0:NS], ident[:, :], start=True, stop=True)
                last.then_inc(S("tok_mm"), 1)

            def transpose_p(j, i):
                nk = i // 2 + 1
                pe.wait_ge(S("p_ready"), 16 * j + i + 1)
                wait(pe, S("pt_ready"), 16 * j + i)
                if i == 0:
                    pe.wait_ge(S("v_hl"), j + 1)
                for k in range(nk):
                    last = nc.tensor.transpose(pair(2)[:, k * P:(k + 1) * P], prob[:, k * P:(k + 1) * P], ident[:, :])
                last.then_inc(S("t_done"), 1)

            def values(j, i):
                nk = i // 2 + 1
                h = i % 2
                pe.wait_ge(S("pt_ready"), 16 * j + i + 1)
                wait(pe, S("o_evac"), 16 * j + max(i - 1, 0))
                out = bank(6 + h)
                for k in range(nk):
                    mm(out[:, 0:2 * HD], pt_hi[:, k, :], Vhl[:, k, h, :, :].rearrange("p a d -> p (a d)"),
                       start=(k == 0), stop=False)
                    last = mm(out[:, 0:HD], pt_lo[:, k, :], Vhl[:, k, h, 0, :], start=False, stop=(k == nk - 1))
                last.then_inc(S("pv_done"), 1)

            for q in range(4):
                for n in range(16):
                    if q == 0 and n == 0:
                        pe.wait_ge(S("f_evac"), 1)
                    step(0, q, n)
            transpose_vt(0)

            def phase(j, par, more):
                for i in range(16):
                    if i >= 1:
                        transpose_p(j, i - 1)
                    scores(j, i, par)
                    before = -(3 * i) % 16
                    first = before if more and 0 < before < 3 else 3
                    if more:
                        for n in range(3 * i, 3 * i + first):
                            step(j + 1, n // 16, n % 16)
                    if i >= 1:
                        values(j, i - 1)
                    if more:
                        for n in range(3 * i + first, 3 * i + 3):
                            step(j + 1, n // 16, n % 16)
                    if not more and i == 0:
                        pe.wait_ge(S("evac"), 12 * KB)
                        turn(1, 0)

                def z_steps(a, b):
                    for n in range(a, b):
                        if more:
                            step(j + 1, 3, n)

                transpose_p(j, 15)
                z_steps(0, 4)
                values(j, 15)
                z_steps(4, 8)
                if more:
                    transpose_vt(j + 1)
                z_steps(8, 12)
                pe.wait_ge(S("o_evac"), 16 * j + 16)
                for t in range(TT):
                    last = nc.tensor.transpose(pair(1)[:, t * P:(t + 1) * P], otok[:, t, :], ident[:, :])
                last.then_inc(S("ot_done"), 1)
                z_steps(12, 16)

            phase(0, 0, True)
            with pe.Fori(0, KB // 2 - 1) as i2:
                phase(2 * i2 + 1, 1, True)
                phase(2 * i2 + 2, 0, True)
            phase(KB - 1, 1, False)

            for b in range(KB):
                slot = (U_FA + b) % 2
                pe.wait_ge(S("lo_ready"), U_FA + b + 1)
                for half in range(2):
                    cs = slice(half * HALF, half * HALF + HALF)
                    if b == 0:
                        pe.wait_ge(S("evac"), 12 * KB)
                    wait(pe, S("fg2_ready"), 2 * b + half - 1)
                    for k in range(KB):
                        if b == 0 and half == 0:
                            pe.wait_ge(S("y2_split"), k + 1)
                        last = three(bank(half), w_hi[:, slot, k, :], w_lo[:, slot, k, :],
                                     y2_hi[:, k, cs], y2_lo[:, k, cs], k == 0, k == KB - 1)
                    last.then_inc(S("fa_mm"), 1)
                if b == 4:
                    turn(1, 2)
                    turn(0, 3)
                if b == 5:
                    pe.wait_ge(S("tok_ready"), 3)
                    turn(2, 2)
                    mm(bank(6)[0:NS, 0:H], fS[:, :], ident[0:H, 0:H], start=True, stop=True).then_inc(S("tok_mm"), 1)
                if b == 6:
                    pe.wait_ge(S("tok_ready"), 4)
                    pe.wait_ge(S("fpg_in"), 16 * NP * NS)
                    for p in range(NP):
                        last = nc.tensor.transpose(bank(4)[:, p * P:(p + 1) * P], fpg[:, p, :, :].rearrange("p b h -> p (b h)"), ident[:, :])
                    last.then_inc(S("d_tr"), 1)
                    pe.wait_ge(S("sn_ready"), 1)
                    for c in range(2):
                        last = mm(bank(6)[:, c:c + 1], ex[:, c, :, :].rearrange("p b h -> p (b h)"), ones[0:NS, 0:1],
                                  start=True, stop=True)
                    last.then_inc(S("d_new"), 1)

            pe.wait_ge(S("pages_used"), NS)
            for p in range(NP):
                last = nc.tensor.transpose(bank(5)[:, p * P:(p + 1) * P], scol[:, p, :, :].rearrange("p b h -> p (b h)"), ident[:, :])
            last.then_inc(S("d_tr"), 1)
            pe.wait_ge(S("r2_ready"), 2 * KB)
            pe.wait_ge(S("fg2_ready"), 2 * KB)
            ln_forward(0, r2T, TT)
            ln_forward(1, r2T, TT)
            pe.wait_ge(S("d_p"), 1)
            for p in range(NP):
                nc.tensor.transpose(bank(4)[:, p * P:(p + 1) * P], Ld[:, p * P:(p + 1) * P], ident[:, :])
            mm(bank(5)[0:NS, 0:P], pdx[:, :], ident[:, :], start=True, stop=True).then_inc(S("d_tr"), 1)
            pe.wait_ge(S("d_pt"), 1)
            for b in range(NS):
                s = b % 4
                pe.wait_ge(S(f"pages_in{s}"), 16 * NP * (b // 4 + (5 if s < 2 else 1)))
                for p in range(NP):
                    for h in range(2):
                        last = mm(bank(6 + h), PZ[:, p, b, :], pages[:, s, p, h * 512:(h + 1) * 512],
                                  start=(b == 0 and p == 0), stop=False)
                last.then_inc(S("pages_used"), 1)
                if b + 2 < TT:
                    ln_forward(b + 2, r2T, TT)
            for h in range(2):
                last = mm(bank(6 + h), pd[:, :], vtok[:, h * 512:(h + 1) * 512], start=False, stop=True)
            last.then_inc(S("d_pv"), 1)
            pe.wait_ge(S("om_ready"), 1)
            for c in range(KB):
                last = mm(bank(4)[:, c * NS:(c + 1) * NS], omask[:, c * P:(c + 1) * P], maskp[:, :], start=True, stop=True)
            last.then_inc(S("d_o"), 1)
            pe.wait_ge(S("os_ready"), 1)
            pe.wait_ge(S("fsw_in"), 16 * KB)
            for h in range(2):
                for k in range(KB):
                    last = mm(bank(6 + h)[0:NS, :], oS[:, k, :], fsw[:, 4 * h:4 * h + 4, k, :], start=(k == 0), stop=(k == KB - 1))
                last.then_inc(S("fs_used"), 1)
            for h in range(2):
                pe.wait_ge(S("fs_row"), h + 1)
                for b in range(4 * h, 4 * h + 4):
                    last = mm(bank(5)[:, b * NS:(b + 1) * NS], fs_row[:, b * P:(b + 1) * P], ident[0:NS, 0:NS], start=True, stop=True)
            last.then_inc(S("fs_used"), 1)
            sample_sums(3)


def kernel(**inputs):
    import numpy as np
    import concourse.bacc as bacc
    from concourse.bass_utils import run_bass_kernel_spmd as run

    x = {k: np.asarray(a) for k, a in inputs.items()}

    def blocks(w):
        k, n = w.shape
        return w.reshape(k // D, KB, P, n // P, P).transpose(3, 0, 2, 1, 4)

    w_in = blocks(x["cm_w_in"][0])[:, 0]
    kv = x["kv_w"]
    w_f = np.concatenate([kv[:, 2 * D:], np.zeros((D, P - H), kv.dtype)], axis=1)
    fa = blocks(x["fa_w_in"][0])[:, 0]
    kvb = blocks(kv[:, :2 * D])[:, 0]
    w_out = blocks(x["cm_w_out"][0])
    units = np.concatenate([
        w_in[WB:2 * WB],
        np.stack([w_in[2 * WB:], w_in[:WB]], axis=1).reshape(2 * WB, P, KB, P),
        w_out.reshape(2 * KB, P, KB, P),
        blocks(w_f)[:, 0],
        np.stack([kvb[:KB], fa[:KB], kvb[KB:], fa[KB:]], axis=1).reshape(4 * KB, P, KB, P),
        blocks(x["fa_w_out"][0])[:, 0],
    ])
    ada = np.concatenate([blocks(w)[:, 0] for w in x["w_ada"]])

    def feature(v):
        return np.ascontiguousarray(v).reshape(-1, P).T

    c9 = np.concatenate([x["c_sample"], x["c_prompt"]])
    x_all = np.concatenate([x["x_prompt"][0], x["x_sample"][:, 0]])
    kb, fb = x["kv_b"], x["fa_b_in"][0]
    b_f = np.concatenate([kb[2 * D:], np.zeros(P - H, kb.dtype)])
    rep = WB // x["cm_w_s"].shape[1]
    w00 = np.broadcast_to(np.repeat(x["cm_w_s"][0, :, 0, 0], rep)[None], (P, WB))
    b00 = np.broadcast_to(np.repeat(x["cm_b_s"][0, :, 0], rep)[None], (P, WB))
    cols = np.concatenate([
        feature(x["b_ada"]), feature(x["cm_b_in"][0]), feature(x["cm_b_out"][0]),
        feature(kb[:D]), feature(fb[:D]), feature(kb[D:2 * D]), feature(fb[D:]), feature(b_f),
        feature(x["fa_b_out"][0]), feature(x["ln_g"]), feature(x["ln_b"]),
        feature(x["cm_ln_v_g"][0]), feature(x["cm_ln_v_b"][0]), w00, b00], axis=1)
    arrays = {
        "units": units,
        "w_ada0": x["w_ada"][0, :, :2 * D].reshape(KB, P, 4, 512).transpose(1, 2, 0, 3),
        "w_ada": ada[16:],
        "c_t": c9.reshape(9, KB, P).transpose(2, 1, 0),
        "x_t": x_all.reshape(TA, KB, P).transpose(2, 1, 0),
        "cols_d": cols,
        "ws_t": x["cm_w_s"][0].transpose(2, 0, 1),
        "bs_row": x["cm_b_s"],
        "ln_rows": np.stack([x["ln_g"][1], x["ln_b"][1]]),
        "table": x["page_table"].reshape(1, NS * NP),
        "cache_k": x["cache_k"].reshape(-1, P, D), "cache_v": x["cache_v"].reshape(-1, P, D),
        "cache_f": x["cache_logf"],
    }
    outs = {"y_out": (T, D), "ys_out": (P, KB, NS), "k_out": (KB, P, T), "v_out": (KB, P, T), "f_out": (H, TA),
            "kqv_s_out": (P, 3, KB, 9), "vn_out": (P, WB, NS)}
    nc = bacc.Bacc("TRN2", target_bir_lowering=False, num_devices=1)
    arrays = {k: np.ascontiguousarray(a) for k, a in arrays.items()}
    args = [nc.dram_tensor(k, a.shape, mybir.dt.from_np(a.dtype), kind="ExternalInput").ap() for k, a in arrays.items()]
    args += [nc.dram_tensor(k, s, F32, kind="ExternalOutput").ap() for k, s in outs.items()]
    trunk(nc, *args)
    r = run(nc, [arrays], core_ids=[0]).results[0]

    def rows(a):
        return np.ascontiguousarray(a.transpose(2, 0, 1)).reshape(1, T, H, HD)

    def decode(a):
        return np.ascontiguousarray(a.transpose(2, 1, 0)).reshape(NS, 1, -1)

    s = r["kqv_s_out"]
    return (r["y_out"].reshape(1, T, D), decode(r["ys_out"]), rows(r["k_out"]), rows(r["v_out"]),
            np.ascontiguousarray(r["f_out"][:, :T].T).reshape(1, T, H),
            decode(s[:, 0, :, :NS]).reshape(NS, 1, H, HD), decode(s[:, 2, :, :NS]).reshape(NS, 1, H, HD),
            np.ascontiguousarray(r["f_out"][:, T:].T).reshape(NS, 1, H),
            decode(r["vn_out"]).reshape(1, NS, 1, W))
```
